# Optimizing a Trainium2 kernel written in Bass

```python
import math
import jax, jax.numpy as jnp
from jax import lax
import numpy as np

D_MODEL = 1024
BATCH = 1
SEQ = 512
DEPTH = 2

NSA_HEADS = 8
NSA_KV_HEADS = 2
NSA_GROUP = NSA_HEADS // NSA_KV_HEADS
HEAD_DIM = 64
ROPE_DIMS = HEAD_DIM // 4
ROPE_THETA = 500000.0
CMP_BLOCK = 32
CMP_STRIDE = 16
CMP_HIDDEN = 2 * HEAD_DIM
SLC_BLOCK = 64
SLC_TOPK = 16
WINDOW = 512
Q_BLOCK = 128
SLC_Q_CHUNK = 32
NSA_WIDTH = NSA_HEADS * HEAD_DIM
KV_WIDTH = NSA_KV_HEADS * HEAD_DIM
S5_WIDTH = 256
S5_GROUP_CH = 16
S5_GROUPS = S5_WIDTH // S5_GROUP_CH
S5_STATE = 64
N_BRANCHES = 2
N_EXPERT_GROUPS = 4
EXPERTS_PER_GROUP = 8
N_EXPERTS = N_EXPERT_GROUPS * EXPERTS_PER_GROUP
EXPERT_TOP_K = 2
EXPERT_FF = 512
MOE_BLOCK = 128
RMS_EPS = 1e-6
NEG_BIG = -1e30
IN_COLS = NSA_WIDTH + 6 * KV_WIDTH + 3 * NSA_HEADS + S5_WIDTH + N_BRANCHES * D_MODEL

kernel_name = 'hybrid_nsa_s5_hiermoe_trunk'

def rmsnorm(x, gain):
    xf = x.astype(jnp.float32)
    xf = xf * lax.rsqrt(jnp.mean(xf * xf, axis=-1, keepdims=True) + RMS_EPS)
    return xf.astype(x.dtype) * gain

def rope_partial(x, pos):
    inv_freq = ROPE_THETA ** (-jnp.arange(0, ROPE_DIMS, 2, dtype=jnp.float32) / ROPE_DIMS)
    ang = pos.astype(jnp.float32)[..., None] * inv_freq
    cos = jnp.cos(ang).astype(x.dtype)
    sin = jnp.sin(ang).astype(x.dtype)
    half = ROPE_DIMS // 2
    x1 = x[..., :half]
    x2 = x[..., half:ROPE_DIMS]
    return jnp.concatenate([x1 * cos - x2 * sin, x2 * cos + x1 * sin, x[..., ROPE_DIMS:]], axis=-1)

def masked_softmax(s, mask):
    s = jnp.where(mask, s.astype(jnp.float32), NEG_BIG)
    return jnp.where(mask, jax.nn.softmax(s, axis=-1), 0.0)

def nsa_mixer(q, k_cmp, v_cmp, k_slc, v_slc, k_win, v_win, gate_logits, positions,
              q_gain, k_gain, ck_pos, ck_w1, ck_w2, cv_pos, cv_w1, cv_w2):
    B, S, _ = q.shape
    Hkv, G, dh = NSA_KV_HEADS, NSA_GROUP, HEAD_DIM
    scale = dh ** -0.5
    t_idx = jnp.arange(S)

    def heads(t, n):
        return t.reshape(B, S, n, dh).transpose(0, 2, 1, 3)

    pos = positions[:, None, :]
    qh = rope_partial(rmsnorm(heads(q, NSA_HEADS), q_gain), pos).reshape(B, Hkv, G, S, dh)

    n_cmp = (S - CMP_BLOCK) // CMP_STRIDE + 1
    blk_idx = np.arange(n_cmp)[:, None] * CMP_STRIDE + np.arange(CMP_BLOCK)[None, :]

    def compress(t, pos_emb, w1, w2):
        blocks = heads(t, Hkv)[:, :, blk_idx] + pos_emb
        flat = blocks.reshape(B, Hkv, n_cmp, CMP_BLOCK * dh)
        return jax.nn.gelu(flat @ w1) @ w2

    cmp_end = blk_idx[:, -1]
    kc = rope_partial(rmsnorm(compress(k_cmp, ck_pos, ck_w1, ck_w2), k_gain), positions[:, cmp_end][:, None, :])
    vc = compress(v_cmp, cv_pos, cv_w1, cv_w2)
    s_c = jnp.einsum('bhgsd,bhcd->bhgsc', qh, kc) * scale
    mask_c = jnp.asarray(cmp_end)[None, :] <= t_idx[:, None]
    p_c = masked_softmax(s_c, mask_c)
    o_c = jnp.einsum('bhgsc,bhcd->bhgsd', p_c.astype(vc.dtype), vc)

    n_slc = S // SLC_BLOCK
    top_k = min(SLC_TOPK, n_slc)
    cmp_start = np.arange(n_cmp) * CMP_STRIDE
    slc_start = np.arange(n_slc) * SLC_BLOCK
    overlap = ((cmp_start[:, None] < slc_start[None, :] + SLC_BLOCK)
               & (cmp_start[:, None] + CMP_BLOCK > slc_start[None, :])).astype(np.float32)
    imp = jnp.einsum('bhgsc,cn->bhsn', p_c, jnp.asarray(overlap))
    j = jnp.arange(n_slc)[None, :]
    cur = (t_idx // SLC_BLOCK)[:, None]
    forced = (j == 0) | (j == cur) | (j == cur - 1)
    imp = jnp.where(forced, jnp.inf, jnp.where(j > cur, -jnp.inf, imp))
    _, sel = lax.top_k(imp, top_k)

    ks_blk = rope_partial(rmsnorm(heads(k_slc, Hkv), k_gain), pos).reshape(B, Hkv, n_slc, SLC_BLOCK, dh)
    vs_blk = heads(v_slc, Hkv).reshape(B, Hkv, n_slc, SLC_BLOCK, dh)
    n_chunk = S // SLC_Q_CHUNK
    q_ch = qh.reshape(B, Hkv, G, n_chunk, SLC_Q_CHUNK, dh).transpose(3, 0, 1, 2, 4, 5)
    sel_ch = sel.reshape(B, Hkv, n_chunk, SLC_Q_CHUNK, top_k).transpose(2, 0, 1, 3, 4)
    t_ch = t_idx.reshape(n_chunk, SLC_Q_CHUNK)
    b_ix = jnp.arange(B)[:, None, None, None]
    h_ix = jnp.arange(Hkv)[None, :, None, None]

    def slc_chunk(args):
        qc, sc, tc = args
        kg = ks_blk[b_ix, h_ix, sc]
        vg = vs_blk[b_ix, h_ix, sc]
        C = tc.shape[0]
        s = jnp.einsum('bhgqd,bhqnkd->bhgqnk', qc, kg).reshape(B, Hkv, G, C, top_k * SLC_BLOCK) * scale
        key_pos = sc[..., None] * SLC_BLOCK + jnp.arange(SLC_BLOCK)
        mask = (key_pos <= tc[None, None, :, None, None]).reshape(B, Hkv, 1, C, top_k * SLC_BLOCK)
        p = masked_softmax(s, mask)
        return jnp.einsum('bhgqm,bhqmd->bhgqd', p.astype(vg.dtype), vg.reshape(B, Hkv, C, top_k * SLC_BLOCK, dh))

    o_s = lax.map(slc_chunk, (q_ch, sel_ch, t_ch))
    o_s = o_s.transpose(1, 2, 3, 0, 4, 5).reshape(B, Hkv, G, S, dh)

    nb = S // Q_BLOCK
    n_prev = WINDOW // Q_BLOCK

    def windows(t):
        tb = jnp.pad(t.reshape(B, Hkv, nb, Q_BLOCK, dh), ((0, 0), (0, 0), (n_prev, 0), (0, 0), (0, 0)))
        return jnp.concatenate([tb[:, :, i:i + nb] for i in range(n_prev + 1)], axis=3)

    kw = windows(rope_partial(rmsnorm(heads(k_win, Hkv), k_gain), pos))
    vw = windows(heads(v_win, Hkv))
    qw = qh.reshape(B, Hkv, G, nb, Q_BLOCK, dh)
    s_w = jnp.einsum('bhgnqd,bhnkd->bhgnqk', qw, kw) * scale
    q_pos = jnp.arange(nb)[:, None] * Q_BLOCK + jnp.arange(Q_BLOCK)[None, :]
    k_pos = (jnp.arange(nb)[:, None] - n_prev) * Q_BLOCK + jnp.arange((n_prev + 1) * Q_BLOCK)[None, :]
    diff = q_pos[:, :, None] - k_pos[:, None, :]
    mask_w = (diff >= 0) & (diff < WINDOW) & (k_pos[:, None, :] >= 0)
    p_w = masked_softmax(s_w, mask_w)
    o_w = jnp.einsum('bhgnqk,bhnkd->bhgnqd', p_w.astype(vw.dtype), vw).reshape(B, Hkv, G, S, dh)

    g = jax.nn.sigmoid(gate_logits.reshape(B, S, NSA_HEADS, 3).transpose(0, 2, 1, 3)).reshape(B, Hkv, G, S, 3)
    o = g[..., 0:1] * o_c + g[..., 1:2] * o_s + g[..., 2:3] * o_w
    return o.transpose(0, 3, 1, 2, 4).reshape(B, S, NSA_WIDTH)

def s5_mixer(u, a_re, a_im, log_dt, b_re, b_im, c_re, c_im, d_skip, w_glu):
    B, S, _ = u.shape
    f32 = jnp.float32
    lam_re = jnp.minimum(a_re.astype(f32), -1e-4)
    lam_im = a_im.astype(f32)
    dt = jnp.exp(log_dt.astype(f32))[:, None]
    mag = jnp.exp(lam_re * dt)
    ang = lam_im * dt
    lb_re = mag * jnp.cos(ang)
    lb_im = mag * jnp.sin(ang)
    den = lam_re * lam_re + lam_im * lam_im
    f_re = ((lb_re - 1.0) * lam_re + lb_im * lam_im) / den
    f_im = (lb_im * lam_re - (lb_re - 1.0) * lam_im) / den
    br = b_re.astype(f32)
    bi = b_im.astype(f32)
    bb_re = f_re[..., None] * br - f_im[..., None] * bi
    bb_im = f_re[..., None] * bi + f_im[..., None] * br
    ug = u.astype(f32).reshape(B, S, S5_GROUPS, S5_GROUP_CH)
    bu_re = jnp.einsum('bsgc,gpc->sbgp', ug, bb_re)
    bu_im = jnp.einsum('bsgc,gpc->sbgp', ug, bb_im)
    a_re_t = jnp.broadcast_to(lb_re, bu_re.shape)
    a_im_t = jnp.broadcast_to(lb_im, bu_im.shape)

    def combine(left, right):
        ar1, ai1, br1, bi1 = left
        ar2, ai2, br2, bi2 = right
        return (ar2 * ar1 - ai2 * ai1, ar2 * ai1 + ai2 * ar1,
                ar2 * br1 - ai2 * bi1 + br2, ar2 * bi1 + ai2 * br1 + bi2)

    _, _, x_re, x_im = lax.associative_scan(combine, (a_re_t, a_im_t, bu_re, bu_im), axis=0)
    y = (jnp.einsum('sbgp,gcp->bsgc', x_re, c_re.astype(f32))
         - jnp.einsum('sbgp,gcp->bsgc', x_im, c_im.astype(f32))).reshape(B, S, S5_WIDTH)
    y = y + d_skip.astype(f32) * ug.reshape(B, S, S5_WIDTH)
    y = jax.nn.gelu(y).astype(u.dtype)
    z = y @ w_glu
    return z[..., :S5_WIDTH] * jax.nn.sigmoid(z[..., S5_WIDTH:])

def hier_moe(h, w_rg, b_rg, w_re, b_re, w_gate, w_up, w_down):
    B, S, D = h.shape
    N = B * S
    ht = h.reshape(N, D)
    g_logits = (ht @ w_rg + b_rg).astype(jnp.float32)
    g_sel = jnp.argmax(g_logits, axis=-1)
    g_w = jnp.take_along_axis(jax.nn.softmax(g_logits, axis=-1), g_sel[:, None], axis=1)
    e_logits = (ht @ w_re + b_re).astype(jnp.float32).reshape(N, N_EXPERT_GROUPS, EXPERTS_PER_GROUP)
    e_logits = jnp.take_along_axis(e_logits, g_sel[:, None, None], axis=1)[:, 0]
    top_p, top_i = lax.top_k(jax.nn.softmax(e_logits, axis=-1), EXPERT_TOP_K)
    w = g_w * top_p / jnp.sum(top_p, axis=-1, keepdims=True)
    expert = g_sel[:, None].astype(jnp.int32) * EXPERTS_PER_GROUP + top_i

    A = N * EXPERT_TOP_K
    e_flat = expert.reshape(A)
    tok = jnp.repeat(jnp.arange(N, dtype=jnp.int32), EXPERT_TOP_K)
    order = jnp.argsort(e_flat)
    e_sorted = e_flat[order]
    tok_sorted = tok[order]
    w_sorted = w.reshape(A)[order]
    counts = jnp.zeros((N_EXPERTS,), jnp.int32).at[e_flat].add(1)
    starts = jnp.cumsum(counts) - counts
    padded = (counts + MOE_BLOCK - 1) // MOE_BLOCK * MOE_BLOCK
    pends = jnp.cumsum(padded)
    pstarts = pends - padded
    dest = pstarts[e_sorted] + (jnp.arange(A, dtype=jnp.int32) - starts[e_sorted])
    cap = A + N_EXPERTS * MOE_BLOCK
    n_blk = cap // MOE_BLOCK
    buf = jnp.zeros((cap, D), h.dtype).at[dest].set(ht[tok_sorted])
    blk_expert = jnp.minimum(jnp.searchsorted(pends, jnp.arange(n_blk) * MOE_BLOCK, side='right'), N_EXPERTS - 1)

    def expert_block(args):
        xb, e = args
        return (jax.nn.silu(xb @ w_gate[e]) * (xb @ w_up[e])) @ w_down[e]

    out_buf = lax.map(expert_block, (buf.reshape(n_blk, MOE_BLOCK, D), blk_expert)).reshape(cap, D)
    y_a = out_buf[dest] * w_sorted[:, None].astype(h.dtype)
    return jax.ops.segment_sum(y_a, tok_sorted, num_segments=N).reshape(B, S, D)

def setup_inputs(seed: int = 0) -> dict:
    key = jax.random.key(seed)
    keys = iter(jax.random.split(key, 48))
    f32 = jnp.float32
    L = DEPTH

    def nrm(shape, scale):
        return jax.random.normal(next(keys), shape, f32) * scale

    res_scale = (2.0 * DEPTH) ** -0.5
    x = nrm((BATCH, SEQ, D_MODEL), 1.0)
    start = jax.random.randint(next(keys), (BATCH, 1), 0, 4096, dtype=jnp.int32)
    positions = start + jnp.arange(SEQ, dtype=jnp.int32)[None, :]
    n_idx = jnp.arange(S5_STATE, dtype=f32)
    return {
        'x': x,
        'positions': positions,
        'norm_mix': 1.0 + nrm((L, D_MODEL), 0.02),
        'norm_ffn': 1.0 + nrm((L, D_MODEL), 0.02),
        'w_in': nrm((L, D_MODEL, IN_COLS), D_MODEL ** -0.5),
        'q_gain': 1.0 + nrm((L, HEAD_DIM), 0.02),
        'k_gain': 1.0 + nrm((L, HEAD_DIM), 0.02),
        'cmp_k_pos': nrm((L, CMP_BLOCK, HEAD_DIM), 0.1),
        'cmp_k_w1': nrm((L, CMP_BLOCK * HEAD_DIM, CMP_HIDDEN), (CMP_BLOCK * HEAD_DIM) ** -0.5),
        'cmp_k_w2': nrm((L, CMP_HIDDEN, HEAD_DIM), CMP_HIDDEN ** -0.5),
        'cmp_v_pos': nrm((L, CMP_BLOCK, HEAD_DIM), 0.1),
        'cmp_v_w1': nrm((L, CMP_BLOCK * HEAD_DIM, CMP_HIDDEN), (CMP_BLOCK * HEAD_DIM) ** -0.5),
        'cmp_v_w2': nrm((L, CMP_HIDDEN, HEAD_DIM), CMP_HIDDEN ** -0.5),
        's5_a_re': -0.5 + nrm((L, S5_GROUPS, S5_STATE), 0.01),
        's5_a_im': math.pi * n_idx + nrm((L, S5_GROUPS, S5_STATE), 0.01),
        's5_log_dt': jax.random.uniform(next(keys), (L, S5_GROUPS), f32, math.log(1e-3), math.log(1e-1)),
        's5_b_re': nrm((L, S5_GROUPS, S5_STATE, S5_GROUP_CH), (2.0 * S5_GROUP_CH) ** -0.5),
        's5_b_im': nrm((L, S5_GROUPS, S5_STATE, S5_GROUP_CH), (2.0 * S5_GROUP_CH) ** -0.5),
        's5_c_re': nrm((L, S5_GROUPS, S5_GROUP_CH, S5_STATE), (2.0 * S5_STATE) ** -0.5),
        's5_c_im': nrm((L, S5_GROUPS, S5_GROUP_CH, S5_STATE), (2.0 * S5_STATE) ** -0.5),
        's5_d': nrm((L, S5_WIDTH), 0.5),
        's5_glu': nrm((L, S5_WIDTH, 2 * S5_WIDTH), S5_WIDTH ** -0.5),
        'proj_nsa': nrm((L, NSA_WIDTH, D_MODEL), NSA_WIDTH ** -0.5),
        'proj_s5': nrm((L, S5_WIDTH, D_MODEL), S5_WIDTH ** -0.5),
        'w_out': nrm((L, D_MODEL, D_MODEL), D_MODEL ** -0.5 * res_scale),
        'router_group': nrm((L, D_MODEL, N_EXPERT_GROUPS), D_MODEL ** -0.5),
        'router_group_bias': nrm((L, N_EXPERT_GROUPS), 0.01),
        'router_expert': nrm((L, D_MODEL, N_EXPERTS), D_MODEL ** -0.5),
        'router_expert_bias': nrm((L, N_EXPERTS), 0.01),
        'expert_gate': nrm((L, N_EXPERTS, D_MODEL, EXPERT_FF), D_MODEL ** -0.5),
        'expert_up': nrm((L, N_EXPERTS, D_MODEL, EXPERT_FF), D_MODEL ** -0.5),
        'expert_down': nrm((L, N_EXPERTS, EXPERT_FF, D_MODEL), EXPERT_FF ** -0.5 * res_scale),
    }

def reference(x, positions, norm_mix, norm_ffn, w_in, q_gain, k_gain,
              cmp_k_pos, cmp_k_w1, cmp_k_w2, cmp_v_pos, cmp_v_w1, cmp_v_w2,
              s5_a_re, s5_a_im, s5_log_dt, s5_b_re, s5_b_im, s5_c_re, s5_c_im, s5_d, s5_glu,
              proj_nsa, proj_s5, w_out, router_group, router_group_bias, router_expert,
              router_expert_bias, expert_gate, expert_up, expert_down):
    sizes = (NSA_WIDTH, KV_WIDTH, KV_WIDTH, KV_WIDTH, KV_WIDTH, KV_WIDTH, KV_WIDTH,
             3 * NSA_HEADS, S5_WIDTH, D_MODEL, D_MODEL)
    split_at = np.cumsum(sizes)[:-1].tolist()
    for l in range(DEPTH):
        h = rmsnorm(x, norm_mix[l])
        z = h @ w_in[l]
        q, kc, vc, ks, vs, kw, vw, nsa_g, u, g_a, g_s = jnp.split(z, split_at, axis=-1)
        o_a = nsa_mixer(q, kc, vc, ks, vs, kw, vw, nsa_g, positions, q_gain[l], k_gain[l],
                        cmp_k_pos[l], cmp_k_w1[l], cmp_k_w2[l], cmp_v_pos[l], cmp_v_w1[l], cmp_v_w2[l])
        o_b = s5_mixer(u, s5_a_re[l], s5_a_im[l], s5_log_dt[l], s5_b_re[l], s5_b_im[l],
                       s5_c_re[l], s5_c_im[l], s5_d[l], s5_glu[l])
        merged = jax.nn.sigmoid(g_a) * (o_a @ proj_nsa[l]) + jax.nn.sigmoid(g_s) * (o_b @ proj_s5[l])
        x = x + merged @ w_out[l]
        x = x + hier_moe(rmsnorm(x, norm_ffn[l]), router_group[l], router_group_bias[l],
                         router_expert[l], router_expert_bias[l],
                         expert_gate[l], expert_up[l], expert_down[l])
    return x


_drawn_inputs = setup_inputs


def setup_inputs(seed=0):
    import zlib

    import numpy as np

    out = dict(_drawn_inputs(seed))
    spreads = {}
    factors = {'norm_mix': 8.0,
     'q_gain': 8.0,
     'k_gain': 8.0,
     'cmp_k_pos': 5.523,
     'cmp_v_pos': 3.126,
     's5_a_re': 64.0,
     's5_a_im': 34.432,
     's5_log_dt': 25.743,
     's5_b_re': 43.984,
     's5_b_im': 39.956,
     's5_c_re': 45.272,
     's5_c_im': 46.072,
     'router_group_bias': 5.915,
     'router_expert_bias': 5.305}
    for name, (base, spread) in spreads.items():
        noise = np.random.default_rng([zlib.crc32(name.encode()), seed]).standard_normal(out[name].shape)
        drawn = base * np.exp(spread * noise) if base else spread * noise
        out[name] = __import__('jax').numpy.asarray(drawn.astype(out[name].dtype))
    for name, factor in factors.items():
        out[name] = (out[name] * factor).astype(out[name].dtype)
    return out
```

```python
from contextlib import ExitStack

import numpy as np

import concourse.bass as bass
from concourse import mybir

F32 = mybir.dt.float32
I32 = mybir.dt.int32
ALU = mybir.AluOpType
ACT = mybir.ActivationFunctionType
AX = mybir.AxisListType

P = 128
D = 1024
S = 512
NT = S // P
KD = D // P
DEPTH = 2
HEADS = 8
KVH = 2
GRP = HEADS // KVH
DH = 64
HALF = 8
NCMP = 31
CSTR = 16
CBLK = 32
NST = 8
SCH = 16
NE = 32
FF = 512
KF = FF // P
CAP = 64
PAIRS = NE // 2
NR = 4 + NE
EPS = 1e-6
BIG = 1e30
SCALE = DH ** -0.5
C_Q, C_KC, C_KS, C_G, C_U, C_GA, C_GS = 0, 512, 768, 1280, 1304, 1560, 2584
CW = 256
TWO_PI = 2 * np.pi
PI_1 = 6.28125
PI_2 = float(np.float32(np.float64(int((TWO_PI - PI_1) * 2 ** 21)) / 2 ** 21))
PI_3 = float(np.float32(TWO_PI - PI_1 - PI_2))
PI_MAX = 3.1415925
ROUND = 12582912.0

CHUNKS = ([("w_in", C_U, KD, CW), ("w_in", C_KC, KD, CW), ("w_in", C_Q, KD, CW), ("w_in", C_Q + CW, KD, CW),
           ("w_in", C_KS, KD, CW), ("w_in", C_KS + CW, KD, CW)]
          + [("w_in", C_GA + CW * j, KD, CW) for j in range(8)]
          + [("proj_s5", 0, 2, D), ("proj_nsa", 0, 4, 512), ("proj_nsa", 512, 4, 512)]
          + [("w_out", CW * j, KD, CW) for j in range(4)])
NRING = 3

SEQ = [("u", 0), ("u", 1), ("s5t", 0), ("bu", 0), ("kc", 0), ("vc", 0), ("bu", 1), ("hid", 0), ("hid", 1)]
SEQ += [("tok", 2, t) for t in range(NT)] + [("y", 0), ("bu", 2)]
SEQ += [("tok", 3, t) for t in range(NT)] + [("cmp", 0), ("cmp", 1), ("y", 1), ("bu", 3)]
SEQ += [("tok", 4, t) for t in range(NT)] + [("y", 2), ("bu", 4)]
SEQ += [("tok", 5, t) for t in range(NT)] + [("ng", 0), ("y", 3), ("bu", 5)]
SEQ += [("gate", 0), ("gate", 1), ("gate", 2), ("y", 4), ("bu", 6), ("gate", 3), ("gate", 4), ("gate", 5), ("y", 5), ("bu", 7)]
SEQ += [("gate", 6), ("gate", 7), ("gate", 8), ("y", 6), ("gate", 9), ("gate", 10), ("gate", 11), ("y", 7)]
SEQ += [("gate", i) for i in range(12, 16)] + [("z", m) for m in range(4)]
SEQ += [x for t in range(NT) for x in (("tq", t), ("tk", t))] + [("tkc", 0)]
GROUPS = [s for s in SEQ if s[0] not in ("s5t", "bu", "y")]
GIDX = {g: i for i, g in enumerate(GROUPS)}
NBANK = 4

CMPB, SLC, WIN = range(3)
UNITS = [(qt, j, br) for qt in range(NT) for j in range(KVH) for br in range(3)]


def key_tiles(unit):
    qt, j, br = unit
    return 1 if br == CMPB else qt + 1


def first_tr(n):
    return sum(key_tiles(u) for u in UNITS[:n])


def trunk(nc, a, out):
    with ExitStack() as ctx:
        def sb(name, shape, dt=F32):
            return ctx.enter_context(nc.sbuf_tensor(name, shape, dt))

        sems = []

        def sem(name, layer=True):
            s = ctx.enter_context(nc.semaphore(name))
            if layer:
                sems.append(s)
            return s

        x = sb("x", [P, NT, D])
        h = sb("h", [P, NT, D])
        hT = sb("hT", [P, KD, S])
        raw = h
        mergedT = hT
        gate_a = sb("gate_a", [P, KD, FF])
        KB = 256
        arena = sb("arena", [P, 130 * KB])

        def view(at_kb, *shape):
            n = int(np.prod(shape))
            v = arena[:, int(at_kb * KB):int(at_kb * KB) + n]
            names = "abcd"[:len(shape)]
            if len(shape) == 1:
                return v
            return v.rearrange(f"p ({' '.join(names)}) -> p {' '.join(names)}", **dict(zip(names, shape)))

        gate_w = [gate_a[:, :, :], view(0, KD, FF)]
        up_w = [view(16, KD, FF), view(32, KD, FF)]
        down_w = [view(48, KF, D), view(64, KF, D)]
        xg = [view(80, KD, CAP), view(82, KD, CAP)]
        actT = [view(84, KF, CAP), view(85, KF, CAP)]
        silu = [view(86, KF, CAP), view(87, KF, CAP)]
        yslot = view(88, D)
        sel = view(92, NT, 2, CAP)
        selw = view(94, NT, 2, CAP)
        selwT = view(96, S)
        ring = [view(8 * i, KD * CW) for i in range(NRING)]
        gates = view(24, 16, S)
        qn = view(56, 2, 12 * DH)
        qT = view(62, GRP, S)
        kT = view(70, 2, S)
        k2 = view(74, 4, S)
        w1 = view(82, 2, 16, P)
        prob = view(74, 2, GRP, S)
        pT = view(90, 4, S)
        zval = view(74, 2, S)
        zsig = view(78, 2, S)
        oT = view(98, GRP, S)
        s5out = view(98, 2, 2, S)
        uT = view(110, 2, S)
        sT = uT
        kcraw, kcn, vcs = (view(106 + i / 2, P) for i in range(3))
        gcmp = view(107.5, 2, 64)
        PAD = 256
        scanbuf = view(114, 4, PAD + S)
        gT = view(126, 2, S)
        junk = view(126, D)

        spare = gate_a[:, :, :].rearrange("p k n -> p (k n)")
        sq = spare[:, 0:D]
        w_glu = spare[:, D:2 * D].rearrange("p (k n) -> p k n", k=2)
        bbt = spare[:, 2 * D:2 * D + 512].rearrange("p (i t c) -> p i t c", i=4, t=NST)
        sbm = spare[:, 2 * D + 512:2 * D + 768].rearrange("p (i t c) -> p i t c", i=2, t=NST)
        bT, cT = (spare[:, 2 * D + 768 + 512 * i:2 * D + 1280 + 512 * i].rearrange("p (i k n) -> p i k n", i=2, k=2)
                  for i in range(2))
        rtmp = spare[:, 2 * D:2 * D + 384].rearrange("p (i g d) -> p i g d", i=4, g=12)
        gsig = spare[:, 3840:3840 + 24 * NT].rearrange("p (t n) -> p t n", t=NT)
        w_ng = view(108, KD, 24)
        w2 = view(109, 2, DH)
        rt = view(100, 8, NT, NE)
        member = view(104, NT, NE)
        wmem = view(104.5, NT, NE)
        slot = view(105, NT, NE)
        lg = view(106, NT, NR)
        ident = sb("ident", [P, P])
        causal = sb("causal", [P, P])
        before = sb("before", [P, P])
        ones = sb("ones", [P, P])
        cmpmask = sb("cmpmask", [P, NT, NCMP + 1])
        some = sb("some", [P, 1])
        iota_i = sb("iota_i", [P, CAP], I32)
        iota = sb("iota", [P, CAP])
        desc = sb("desc", [P, NE])
        thr = sb("thr", [P, 8])
        invf = sb("invf", [P, HALF])
        pos_i = sb("pos_i", [P, 5], I32)
        posf = sb("posf", [P, 5])
        ang = sb("ang", [P, 5, HALF])
        angk = sb("angk", [P, 5, HALF])
        angc = sb("angc", [P, 5, HALF])
        cost = sb("cost", [P, 5, HALF])
        sint = sb("sint", [P, 5, HALF])
        g_mix = sb("g_mix", [P, KD])
        g_ffn = sb("g_ffn", [P, KD])
        q_gain = sb("q_gain", [P, DH])
        k_gain = sb("k_gain", [P, DH])
        cpos = sb("cpos", [P, 2, CSTR])
        w_r = sb("w_r", [P, KD, NR])
        b_r = sb("b_r", [P, NR])
        sa = sb("sa", [P, 3, NST])
        scm = sb("scm", [P, 2, 2, P])
        sd = sb("sd", [P, 2])
        s5v = sb("s5v", [P, 24, NST])
        pw = sb("pw", [P, 9, 3, NST])
        bbw = sb("bbw", [P, 2, NST, 2 * SCH])
        stat = sb("stat", [P, 3, 4])
        qstat = sb("qstat", [P, 3, 66])
        hb = sb("hb", [P, 2])
        kcT = sb("kcT", [P, NCMP + 1])
        nmax = sb("nmax", [P, 2, GRP])
        nbias = sb("nbias", [P, 2, GRP])
        rsum = sb("rsum", [P, 2, GRP])
        rscale = sb("rscale", [P, 2, GRP])
        rs = sb("rs", [P, 12, NT])
        pair = sb("pair", [P, 2, NT, 2])
        cnt = sb("cnt", [P, 10])
        rounds = sb("rounds", [P, 1], I32)
        bank = ctx.enter_context(nc.psum_tensor("bank", [P, 8, 512], F32))

        x_in = sem("x_in", False)
        pool_const = sem("pool_const", False)
        dve_const = sem("dve_const", False)
        rope_angle = sem("rope_angle", False)
        rope_done = sem("rope_done", False)
        arrived = sem("arrived", False)
        cleared = sem("cleared", False)
        tick = sem("tick", False)
        out_sem = sem("out_sem", False)
        ring_in = [sem(f"ring_in{i}") for i in range(NRING)]
        s5_in = sem("s5_in")
        mix_in = sem("mix_in")
        norm = {}
        for w in ("mix", "ffn"):
            for n in ("sums", "mean", "root", "h", "tr", "hT"):
                norm[w, n] = sem(f"{w}_{n}")
        pj_done = sem("pj_done")
        pj_evac = sem("pj_evac")
        s5_dt = sem("s5_dt")
        s5_ang = sem("s5_ang")
        s5_trig = sem("s5_trig")
        bb_ready = sem("bb_ready")
        s5_tr = sem("s5_tr")
        s5_mat = sem("s5_mat")
        bu_done = sem("bu_done")
        bu_copied = sem("bu_copied")
        scan_done = sem("scan_done")
        y_done = sem("y_done")
        ypre_ready = sem("ypre_ready")
        gelu_done = sem("gelu_done")
        sT_ready = sem("sT_ready")
        qk_mean = sem("qk_mean")
        qk_root = sem("qk_root")
        qk_ready = sem("qk_ready")
        kcn_ready = sem("kcn_ready")
        score_done = sem("score_done")
        max_ready = sem("max_ready")
        exp_done = sem("exp_done")
        p_ready = sem("p_ready")
        tr_done = sem("tr_done")
        evac_act = sem("evac_act")
        evac_dve = sem("evac_dve")
        pv_done = sem("pv_done")
        o_evac = sem("o_evac")
        merge_mm = sem("merge_mm")
        merged = sem("merged")
        out_mm = sem("out_mm")
        x_mixed = sem("x_mixed")
        logit_mm = sem("logit_mm")
        r_exp_in = sem("r_exp_in")
        r_exp = sem("r_exp")
        r_member = sem("r_member")
        prefix_mm = sem("prefix_mm")
        rounds_ready = sem("rounds_ready")
        gate_in = [sem(f"gate_in{i}") for i in range(2)]
        up_in = [sem(f"up_in{i}") for i in range(2)]
        down_in = [sem(f"down_in{i}") for i in range(2)]
        gate_free = [sem(f"gate_free{i}") for i in range(2)]
        up_free = [sem(f"up_free{i}") for i in range(2)]
        down_free = [sem(f"down_free{i}") for i in range(2)]
        sel_ready = sem("sel_ready")
        xg_done = sem("xg_done")
        xg_ready = sem("xg_ready")
        swt_tr = sem("swt_tr")
        swt_ready = sem("swt_ready")
        silu_done = sem("silu_done")
        act_ready = sem("act_ready")
        y_ready = sem("y_ready")
        put_mm = sem("put_mm")
        put_add = sem("put_add")
        act_chain = sem("act_chain")
        dve_chain = sem("dve_chain")
        dve_loop = sem("dve_loop")

        N_POOL = 13
        N_DVE_CONST = 9

        def last_use(c):
            if c < 6:
                return pj_done, GIDX[[("u", 1), ("vc", 0)][c] if c < 2 else ("tok", c, NT - 1)] + 1
            if c < 14:
                return pj_done, GIDX[("gate", 2 * (c - 6) + 1)] + 1
            if c < 17:
                return merge_mm, KD // 2 if c == 15 else KD
            return out_mm, NT * (c - 16)

        class Chain:

            def __init__(self, eng, s):
                self.eng, self.s, self.n = eng, s, 0

            def __call__(self, ins):
                ins.then_inc(self.s, 1)
                self.n += 1
                return self.n

            def sync(self, n=None):
                self.eng.wait_ge(self.s, self.n if n is None else n)

            def do(self, ins):
                self(ins)
                self.sync()

        def wait_reg(eng, s, value):
            eng.wait_ge(s, value)
            eng.sem_inc(tick, 1)

        def close_layer(eng, l):
            eng.drain().then_inc(arrived, 1)
            wait_reg(eng, cleared, l + 1)

        def lay(name, l):
            ap = a[name]
            if len(ap.shape) == 2:
                return ap[bass.ds(l, 1), :].rearrange("o n -> (o n)")
            if len(ap.shape) == 3:
                return ap[bass.ds(l, 1), :, :].rearrange("o m n -> (o m) n")
            return ap[bass.ds(l, 1), :, :, :].rearrange("o g m n -> (o g) m n")

        block = ctx.enter_context(nc.Block())

        @block.gpsimd
        def _(pool):
            n = [0]

            def step(ins):
                ins.then_inc(pool_const, 1)
                n[0] += 1

            step(pool.memset(ident[:, :], 0.0))
            step(pool.memset(causal[:, :], 0.0))
            step(pool.memset(before[:, :], 1.0))
            step(pool.memset(cmpmask[:, :, :], 0.0))
            step(pool.memset(some[:, :], 1.0))
            step(pool.iota(iota_i[:, :], [[1, CAP]], base=0, channel_multiplier=0))
            pool.wait_ge(pool_const, n[0])
            step(pool.affine_select(out=ident[:, :], in_=ident[:, :], compare_op=ALU.not_equal, fill=1.0,
                                    base=0, pattern=[[-1, P]], channel_multiplier=1))
            step(pool.affine_select(out=causal[:, :], in_=causal[:, :], compare_op=ALU.is_ge, fill=-BIG,
                                    base=0, pattern=[[-1, P]], channel_multiplier=1))
            step(pool.affine_select(out=before[:, :], in_=before[:, :], compare_op=ALU.is_gt, fill=0.0,
                                    base=0, pattern=[[1, P]], channel_multiplier=-1))
            step(pool.affine_select(out=cmpmask[:, :, :], in_=cmpmask[:, :, :], compare_op=ALU.is_ge, fill=-BIG,
                                    base=-(CBLK - 1), pattern=[[P, NT], [-CSTR, NCMP + 1]], channel_multiplier=1))
            step(pool.affine_select(out=some[:, :], in_=some[:, :], compare_op=ALU.is_ge, fill=0.0,
                                    base=-(CBLK - 1), pattern=[[0, 1]], channel_multiplier=1))
            step(pool.memset(ones[:, :], 1.0))
            step(pool.memset(qstat[:, :, :], 1.0))
            assert n[0] == N_POOL
            with pool.Fori(0, DEPTH) as l:
                wait_reg(pool, arrived, (l + 1) * 4)
                for s in sems:
                    pool.sem_clear(s)
                pool.sem_inc(cleared, 1)

        @block.sync
        def _(sp):
            sp.dma_start(x[:, :, :], a["x"][0].rearrange("(t p) d -> p t d", p=P)).then_inc(x_in, 16)
            sp.wait_ge(dve_const, N_DVE_CONST)
            sp.dma_start(pos_i[:, 0:NT], a["positions"][0].rearrange("(t p) -> p t", p=P),
                         allow_slow_non_contiguous=True).then_inc(x_in, 16)
            sp.dma_start(pos_i[0:NCMP, NT:NT + 1],
                         a["positions"][0, CBLK - 1:S].rearrange("(c o) -> c o", o=1)[0:(NCMP - 1) * CSTR + 1:CSTR, :],
                         allow_slow_non_contiguous=True).then_inc(x_in, 16)
            with sp.Fori(0, DEPTH) as l:
                def small(s, dst, src):
                    sp.dma_start(dst, src, allow_slow_non_contiguous=True).then_inc(s, 16)

                def weights(c):
                    name, col, k, n = CHUNKS[c]
                    if c >= NRING:
                        sp.wait_ge(*last_use(c - NRING))
                    dst = ring[c % NRING].rearrange("p (k n) -> p k n", k=k)
                    if name == "proj_nsa":
                        src = lay(name, l)[:, col:col + n].rearrange("(j g d) n -> j d g n", j=KVH, g=GRP)
                        for j in range(KVH):
                            for g in range(GRP):
                                sp.dma_start(dst[DH * j:DH * j + DH, g, :], src[j, :, g, :]).then_inc(ring_in[c % NRING], 16)
                    else:
                        src = lay(name, l)[:, col:col + n].rearrange("(k p) n -> p k n", p=P)
                        sp.dma_start(dst, src).then_inc(ring_in[c % NRING], 16)

                small(mix_in, g_mix[:, :], lay("norm_mix", l).rearrange("(k p) -> p k", p=P))
                small(mix_in, g_ffn[:, :], lay("norm_ffn", l).rearrange("(k p) -> p k", p=P))
                weights(0)
                for i, name in enumerate(("s5_a_re", "s5_a_im")):
                    small(s5_in, sa[:, i, :], lay(name, l).rearrange("(t g) n -> (g n) t", g=2))
                dts = lay("s5_log_dt", l).rearrange("(t g) -> g t", g=2)
                for g in range(2):
                    small(s5_in, sa[DH * g:DH * g + DH, 2, :], dts[g:g + 1, :].broadcast_to([DH, NST]))
                for i, name in enumerate(("s5_b_re", "s5_b_im")):
                    small(s5_in, sbm[:, i, :, :], lay(name, l).rearrange("(t g) n c -> (g n) t c", g=2))
                for i, name in enumerate(("s5_c_re", "s5_c_im")):
                    cv = lay(name, l).rearrange("(k j g) c n -> k j g c n", k=2, g=2)
                    for k in range(2):
                        for j in range(4):
                            for g in range(2):
                                r = 32 * j + SCH * g
                                small(s5_in, scm[r:r + SCH, i, k, DH * g:DH * g + DH], cv[k, j, g])
                small(s5_in, sd[:, :], lay("s5_d", l).rearrange("(k p) -> p k", p=P))
                weights(1)
                for i, c in enumerate("kv"):
                    for m in range(0, CSTR, 8):
                        small(mix_in, w1[:, i, m:m + 8, :],
                              lay(f"cmp_{c}_w1", l).rearrange("(m p) n -> p m n", p=P)[:, m:m + 8, :])
                    small(mix_in, cpos[:, i, :], lay(f"cmp_{c}_pos", l).rearrange("(m e) d -> (e d) m", e=2))
                    small(mix_in, w2[:, i, :], lay(f"cmp_{c}_w2", l))
                small(mix_in, w_ng[:, :, :], lay("w_in", l)[:, C_G:C_G + 24].rearrange("(k p) n -> p k n", p=P))
                small(mix_in, q_gain[:, :], lay("q_gain", l).partition_broadcast(P))
                small(mix_in, k_gain[:, :], lay("k_gain", l).partition_broadcast(P))
                small(mix_in, w_r[:, :, 0:4], lay("router_group", l).rearrange("(k p) n -> p k n", p=P))
                small(mix_in, w_r[:, :, 4:NR], lay("router_expert", l).rearrange("(k p) n -> p k n", p=P))
                small(mix_in, b_r[:, 0:4], lay("router_group_bias", l).partition_broadcast(P))
                small(mix_in, b_r[:, 4:NR], lay("router_expert_bias", l).partition_broadcast(P))
                small(mix_in, w_glu, lay("s5_glu", l).rearrange("(k p) n -> p k n", p=P))
                for c in range(2, len(CHUNKS)):
                    weights(c)

                sp.wait_ge(x_mixed, 4 * NT)
                sp.wait_ge(rounds_ready, 1)
                nb = sp.value_load(rounds[0:1, 0:1], min_val=1, max_val=S // CAP)
                with sp.Fori(0, nb) as b:
                    with sp.Fori(0, PAIRS) as p:
                        it = b * PAIRS + p
                        for e in range(2):
                            row = (l * NE + p * 2 + e)
                            for name, dst, free, landed in (("expert_gate", gate_w[e], gate_free[e], gate_in[e]),
                                                            ("expert_up", up_w[e], up_free[e], up_in[e]),
                                                            ("expert_down", down_w[e], down_free[e], down_in[e])):
                                src = a[name][bass.ds(row, 1), :, :].rearrange("o (k p) n -> p (o k) n", p=P)
                                wait_reg(sp, free, it + 1)
                                sp.dma_start(dst, src).then_inc(landed, 16)
                close_layer(sp, l)
            sp.dma_start(out[0].rearrange("(t p) d -> p t d", p=P), x[:, :, :]).then_inc(out_sem, 16)
            sp.wait_ge(out_sem, 16)

        N_S5_IN = 16 * (2 + 2 + 2 + 32 // 2 * 2 + 1)
        N_MIX_IN = 16 * (2 + 8 + 1 + 2 + 2 + 2 + 1)

        def ring_count(c):
            return sum(16 * HEADS if CHUNKS[i][0] == "proj_nsa" else 16 for i in range(c % NRING, c + 1, NRING))

        @block.tensor
        def _(pe):
            def chunk(c):
                pe.wait_ge(ring_in[c % NRING], ring_count(c))
                return ring[c % NRING].rearrange("p (k n) -> p k n", k=CHUNKS[c][2])

            def turn(which):
                for t in range(NT):
                    pe.wait_ge(norm[which, "h"], t + 1)
                    for q in range(2):
                        i = 2 * t + q
                        if i >= 4:
                            pe.wait_ge(norm[which, "hT"], i - 3)
                        for k in range(4):
                            m = pe.transpose(bank[:, i % 4, P * k:P * k + P],
                                             h[:, t, P * (4 * q + k):P * (4 * q + k) + P], ident[:, :])
                        m.then_inc(norm[which, "tr"], 1)

            def mm(dst, pairs):
                for i, (w, m) in enumerate(pairs):
                    r = pe.matmul(dst, w, m, start=(i == 0), stop=(i == len(pairs) - 1))
                return r

            def group(g):
                i = GIDX[g]
                if i >= NBANK:
                    pe.wait_ge(pj_evac, i - NBANK + 1)
                b = bank[:, i % NBANK, :]
                kind = g[0]
                if kind == "u":
                    w = chunk(0)
                    r = mm(b, [(w[:, k, P * g[1]:P * g[1] + P], hT[:, k, :]) for k in range(KD)])
                elif kind in ("kc", "vc"):
                    w = chunk(1)
                    o = P * (kind == "vc")
                    r = mm(b, [(w[:, k, o:o + P], hT[:, k, :]) for k in range(KD)])
                elif kind == "tok":
                    w = chunk(g[1])
                    r = mm(b[:, 0:CW], [(hT[:, k, P * g[2]:P * g[2] + P], w[:, k, :]) for k in range(KD)])
                elif kind == "ng":
                    for t in range(NT):
                        r = mm(b[:, 24 * t:24 * t + 24],
                               [(hT[:, k, P * t:P * t + P], w_ng[:, k, :]) for k in range(KD)])
                elif kind == "gate":
                    w = chunk(6 + g[1] // 2)
                    o = P * (g[1] % 2)
                    r = mm(b, [(w[:, k, o:o + P], hT[:, k, :]) for k in range(KD)])
                elif kind == "hid":
                    pe.wait_ge(mix_in, N_MIX_IN)
                    pe.wait_ge(pj_evac, GIDX[("vc" if g[1] else "kc", 0)] + 1)
                    for hh in range(KVH):
                        src = k2[:, 2 * g[1] + hh, :]
                        r = mm(b[:, NCMP * hh:NCMP * hh + NCMP],
                               [(w1[:, g[1], m, :], src[:, 2 * m:2 * m + CSTR * (NCMP - 1) + 1:CSTR]) for m in range(CSTR)])
                    r = mm(b[:, 2 * NCMP:2 * NCMP + 1],
                           [(w1[:, g[1], m, :], cpos[:, g[1], m:m + 1]) for m in range(CSTR)])
                elif kind == "cmp":
                    pe.wait_ge(pj_evac, GIDX[("hid", g[1])] + 1)
                    for hh in range(KVH):
                        r = mm(b[0:NCMP, DH * hh:DH * hh + DH],
                               [(gcmp[:, g[1], NCMP * hh:NCMP * hh + NCMP], w2[:, g[1], :])])
                elif kind == "tq":
                    t = g[1]
                    pe.wait_ge(qk_ready, t + 1)
                    for k in range(GRP):
                        r = pe.transpose(b[:, P * k:P * k + P], qn[:, t % 2, P * k:P * k + P], ident[:, :])
                elif kind == "tk":
                    t = g[1]
                    for k in range(2):
                        r = pe.transpose(b[:, P * k:P * k + P], qn[:, t % 2, 512 + P * k:512 + P * k + P], ident[:, :])
                elif kind == "tkc":
                    pe.wait_ge(kcn_ready, 1)
                    r = pe.transpose(b[:, 0:NCMP], kcn[0:NCMP, :], ident[0:NCMP, 0:NCMP])
                elif kind == "z":
                    pe.wait_ge(gelu_done, 2)
                    m = g[1]
                    r = mm(b, [(w_glu[:, k, P * m:P * m + P], gT[:, k, :]) for k in range(2)])
                r.then_inc(pj_done, 1)

            def s5_step(g):
                kind, t = g
                if kind == "s5t":
                    pe.wait_ge(bb_ready, 4)
                    pe.wait_ge(s5_in, N_S5_IN)
                    for i in range(2):
                        for k in range(2):
                            c = P * (2 * i + k)
                            pe.transpose(bank[:, 4, c:c + P],
                                         bbw[:, i, 4 * k:4 * k + 4, :].rearrange("p a b -> p (a b)"), ident[:, :])
                    for i in range(2):
                        for k in range(2):
                            c = P * (2 * i + k)
                            r = pe.transpose(bank[:, 5, c:c + P], scm[:, i, k, :], ident[:, :])
                    r.then_inc(s5_tr, 1)
                    return
                k, r0 = t // 4, 32 * (t % 4)
                if kind == "bu":
                    if t == 0:
                        pe.wait_ge(s5_mat, 3)
                        pe.wait_ge(pj_evac, 2)
                    else:
                        pe.wait_ge(bu_copied, t)
                    for i in range(2):
                        r = pe.matmul(bank[:, 4 + i, :], bT[r0:r0 + 32, i, k, :], uT[r0:r0 + 32, k, :],
                                      start=True, stop=True, tile_position=(r0, 0))
                    r.then_inc(bu_done, 1)
                else:
                    pe.wait_ge(scan_done, t + 1)
                    for i in range(2):
                        r = pe.matmul(bank[r0:r0 + 32, 6 + k, :], cT[:, i, k, r0:r0 + 32], s5out[:, t % 2, i, :],
                                      start=(i == 0), stop=(i == 1))
                    r.then_inc(y_done, 1)

            def scores(n):
                qt, j, br = UNITS[n]
                nk = NCMP if br == CMPB else P * (qt + 1)
                keys = kcT[:, 0:NCMP] if br == CMPB else kT[:, br - 1, 0:nk]
                for g in range(GRP):
                    if n:
                        pe.wait_ge(exp_done, GRP * (n - 1) + g + 1)
                    rows = slice(DH * j, DH * j + DH)
                    pe.matmul(bank[:, g, 0:nk], qT[rows, g, P * qt:P * qt + P], keys[rows, :], start=True, stop=False)
                    if br == CMPB:
                        r = pe.matmul(bank[:, g, 0:nk], ident[:, :], cmpmask[:, qt, 0:NCMP], start=False, stop=True)
                    else:
                        r = pe.matmul(bank[:, g, P * qt:nk], ident[:, :], causal[:, :], start=False, stop=True)
                    r.then_inc(score_done, 1)

            def values(n):
                qt, j, br = UNITS[n]
                c0 = first_tr(n)
                nt = key_tiles(UNITS[n])
                w = NCMP if br == CMPB else P
                u = n // 3

                def turn_tile(kt):
                    c = c0 + kt
                    if c >= 2:
                        pe.wait_ge(evac_act if c % 2 == 0 else evac_dve, c // 2)
                    for g in range(GRP):
                        if kt == 0:
                            pe.wait_ge(p_ready, GRP * n + g + 1)
                        r = pe.transpose(bank[0:w, 4 + c % 2, P * g:P * g + P],
                                         prob[:, n % 2, g, P * kt:P * kt + w], ident[:, :])
                    r.then_inc(tr_done, 1)

                def add_tile(kt):
                    c = c0 + kt
                    pe.wait_ge(evac_act if c % 2 == 0 else evac_dve, c // 2 + 1)
                    v = (vcs[0:NCMP, DH * j:DH * j + DH] if br == CMPB else
                         raw[:, kt, 640 + 256 * (br - 1) + DH * j:640 + 256 * (br - 1) + DH * j + DH])
                    r = pe.matmul(bank[DH * j:DH * j + DH, 6 + u % 2, :], v, pT[0:w, c % 4, :],
                                  start=(br == CMPB), stop=(br == WIN and kt == nt - 1))
                    r.then_inc(pv_done, 1)

                if br == CMPB and u >= 2:
                    pe.wait_ge(o_evac, u - 1)
                turn_tile(0)
                for kt in range(nt):
                    if kt + 1 < nt:
                        turn_tile(kt + 1)
                    add_tile(kt)

            def merge():
                ws = chunk(14)
                for m in range(KD):
                    wa = chunk(15 + m // 4)
                    o = P * (m % 4)
                    if m >= 2:
                        pe.wait_ge(merged, m - 1)
                    mm(bank[:, 2 * (m % 2), :], [(wa[:, k, o:o + P], oT[:, k, :]) for k in range(4)])
                    r = mm(bank[:, 2 * (m % 2) + 1, :], [(ws[:, k, P * m:P * m + P], sT[:, k, :]) for k in range(2)])
                    r.then_inc(merge_mm, 1)

            def project_out():
                pe.wait_ge(merged, KD)
                for j in range(4):
                    w = chunk(17 + j)
                    for t in range(NT):
                        i = NT * j + t
                        if i >= 4:
                            pe.wait_ge(x_mixed, i - 3)
                        r = mm(bank[:, 4 + i % 4, 0:CW],
                               [(mergedT[:, k, P * t:P * t + P], w[:, k, :]) for k in range(KD)])
                        r.then_inc(out_mm, 1)

            def route():
                pe.wait_ge(norm["ffn", "hT"], 8)
                pe.wait_ge(mix_in, N_MIX_IN)
                for t in range(NT):
                    r = mm(bank[:, 4, NR * t:NR * t + NR],
                           [(hT[:, k, P * t:P * t + P], w_r[:, k, :]) for k in range(KD)])
                r.then_inc(logit_mm, 1)
                pe.wait_ge(r_member, 2)
                for t in range(NT):
                    mm(bank[:, 5, NE * t:NE * t + NE],
                       [(ones[:, :], member[:, i, :]) for i in range(t)] + [(before[:, :], member[:, t, :])])
                r = mm(bank[:, 5, NE * NT:NE * NT + NE], [(ones[:, :], member[:, i, :]) for i in range(NT)])
                r.then_inc(prefix_mm, 1)

            def put(base):
                for s in range(2 * NT):
                    t, half = s // 2, s % 2
                    wait_reg(pe, put_add, base + (s + 1))
                    r = pe.matmul(bank[:, 6 + s % 2, :], selwT[:, P * t:P * t + P],
                                  yslot[:, 512 * half:512 * half + 512], start=True, stop=True)
                    r.then_inc(put_mm, 1)

            def experts():
                pe.wait_ge(rounds_ready, 1)
                nb = pe.value_load(rounds[0:1, 0:1], min_val=1, max_val=S // CAP)
                for e in range(2):
                    for s in (gate_free[e], up_free[e], down_free[e]):
                        pe.sem_inc(s, 1)
                with pe.Fori(0, nb) as b:
                    with pe.Fori(0, PAIRS) as p:
                        it = b * PAIRS + p
                        wait_reg(pe, sel_ready, it + 1)
                        for e in range(2):
                            for k in range(KD):
                                r = mm(bank[:, e, CAP * k:CAP * k + CAP],
                                       [(h[:, t, P * k:P * k + P], sel[:, t, e, :]) for t in range(NT)])
                            r.then_inc(xg_done, 1)
                        wait_reg(pe, swt_ready, it + 1)
                        wait_reg(pe, y_ready, it + 1)
                        put(it * 8)
                        for t in range(NT):
                            r = pe.transpose(bank[:, 4, P * t:P * t + P],
                                             selw[:, t, :, :].rearrange("p e c -> p (e c)"), ident[:, :])
                        r.then_inc(swt_tr, 1)
                        for e in range(2):
                            wait_reg(pe, xg_ready, it * 2 + (e + 1))
                            for w, landed, free, o in ((gate_w[e], gate_in[e], gate_free[e], 0),
                                                       (up_w[e], up_in[e], up_free[e], KF)):
                                wait_reg(pe, landed, it * 16 + 16)
                                for f in range(KF):
                                    r = mm(bank[:, 2 + e, CAP * (o + f):CAP * (o + f) + CAP],
                                           [(w[:, k, P * f:P * f + P], xg[e][:, k, :]) for k in range(KD)])
                                r.then_inc(free, 1)
                        wait_reg(pe, swt_ready, it + 2)
                        for e in range(2):
                            wait_reg(pe, act_ready, it * 2 + (e + 1))
                            wait_reg(pe, down_in[e], it * 16 + 16)
                            for half in range(2):
                                r = mm(bank[CAP * e:CAP * e + CAP, 4 + half, :],
                                       [(actT[e][:, f, :], down_w[e][:, f, 512 * half:512 * half + 512])
                                        for f in range(KF)])
                            r.then_inc(down_free[e], 1)
                wait_reg(pe, swt_ready, nb * PAIRS + 1)
                wait_reg(pe, y_ready, nb * PAIRS + 1)
                put(nb * (PAIRS * 8))

            pe.wait_ge(pool_const, N_POOL)
            pe.wait_ge(dve_const, N_DVE_CONST)
            with pe.Fori(0, DEPTH) as l:
                turn("mix")
                pe.wait_ge(norm["mix", "hT"], 8)
                for g in SEQ:
                    if g[0] in ("s5t", "bu", "y"):
                        s5_step(g)
                    else:
                        group(g)
                pe.wait_ge(pj_evac, len(GROUPS))
                scores(0)
                for n in range(len(UNITS)):
                    if n + 1 < len(UNITS):
                        scores(n + 1)
                    values(n)
                pe.wait_ge(o_evac, 8)
                pe.wait_ge(sT_ready, 2)
                merge()
                project_out()
                turn("ffn")
                route()
                experts()
                close_layer(pe, l)

        @block.scalar
        def _(act):
            def sums(which):
                for t in range(NT):
                    if which == "ffn":
                        act.wait_ge(x_mixed, 3 * NT + t + 1)
                    if t:
                        act.wait_ge(norm[which, "sums"], t)
                    act.activation(junk, x[:, t, :], ACT.Square, accum_out=stat[:, 0, t:t + 1])\
                       .then_inc(norm[which, "sums"], 1)
                act.wait_ge(norm[which, "mean"], 1)
                act.activation(stat[:, 2, :], stat[:, 1, :], ACT.Sqrt).then_inc(norm[which, "root"], 1)

            def evac(g):
                i = GIDX[g]
                act.wait_ge(pj_done, i + 1)
                b = bank[:, i % NBANK, :]
                kind = g[0]
                if kind == "u":
                    r = act.activation(uT[:, g[1], :], b, ACT.Copy)
                elif kind in ("kc", "vc"):
                    o = 2 * (kind == "vc")
                    for hh in range(KVH):
                        rows = slice(DH * hh, DH * hh + DH)
                        act.activation(k2[0:DH, o + hh, :], b[rows, :], ACT.Copy)
                        r = act.activation(k2[DH:P, o + hh, 0:S - 1], b[rows, 1:S], ACT.Copy)
                elif kind == "tok":
                    r = act.activation(raw[:, g[2], CW * (g[1] - 2):CW * (g[1] - 1)], b[:, 0:CW], ACT.Copy)
                elif kind == "ng":
                    r = act.activation(gsig.rearrange("p t n -> p (t n)"), b[:, 0:24 * NT], ACT.Sigmoid)
                elif kind == "gate":
                    r = act.activation(gates[:, g[1], :], b, ACT.Sigmoid)
                elif kind == "hid":
                    act.activation(hb[:, g[1]:g[1] + 1], b[:, 2 * NCMP:2 * NCMP + 1], ACT.Copy).then_inc(act_chain, 1)
                    act.wait_ge(act_chain, g[1] + 1)
                    r = act.activation(gcmp[:, g[1], 0:2 * NCMP], b[:, 0:2 * NCMP], ACT.Gelu_apprx_tanh,
                                       bias=hb[:, g[1]:g[1] + 1])
                elif kind == "cmp":
                    r = act.activation((kcraw if g[1] == 0 else vcs)[0:NCMP, :], b[0:NCMP, 0:P], ACT.Copy)
                elif kind == "tq":
                    r = act.activation(qT[:, :, P * g[1]:P * g[1] + P], b.rearrange("p (g t) -> p g t", g=GRP), ACT.Copy)
                elif kind == "tk":
                    r = act.activation(kT[:, :, P * g[1]:P * g[1] + P],
                                       b[:, 0:2 * P].rearrange("p (g t) -> p g t", g=2), ACT.Copy)
                elif kind == "tkc":
                    r = act.activation(kcT[:, 0:NCMP], b[:, 0:NCMP], ACT.Copy)
                elif kind == "z":
                    if g[1] < 2:
                        r = act.activation(zval[:, g[1], :], b, ACT.Copy)
                    else:
                        r = act.activation(zsig[:, g[1] - 2, :], b, ACT.Sigmoid)
                r.then_inc(pj_evac, 1)

            def exps(n):
                qt, j, br = UNITS[n]
                nk = NCMP if br == CMPB else P * (qt + 1)
                if n == 0:
                    act.wait_ge(sT_ready, 2)
                if n >= 2:
                    act.wait_ge(tr_done, first_tr(n - 1))
                for g in range(GRP):
                    act.wait_ge(max_ready, GRP * n + g + 1)
                    act.activation(prob[:, n % 2, g, 0:nk], bank[:, g, 0:nk], ACT.Exp, scale=SCALE,
                                   bias=nbias[:, n % 2, g:g + 1], accum_out=rsum[:, n % 2, g:g + 1])\
                       .then_inc(exp_done, 1)

            def evac_probs(n):
                qt, j, br = UNITS[n]
                w = NCMP if br == CMPB else P
                for kt in range(key_tiles(UNITS[n])):
                    c = first_tr(n) + kt
                    if c % 2:
                        continue
                    act.wait_ge(tr_done, c + 1)
                    if c >= 4:
                        act.wait_ge(pv_done, c - 3)
                    act.activation(pT[0:w, c % 4, :], bank[0:w, 4, :], ACT.Copy).then_inc(evac_act, 1)
                if br == WIN:
                    act.wait_ge(pv_done, first_tr(n + 1))
                    rows = slice(DH * j, DH * j + DH)
                    act.activation(oT[rows, :, P * qt:P * qt + P],
                                   bank[rows, 6 + (n // 3) % 2, :].rearrange("p (g t) -> p g t", g=GRP), ACT.Copy)\
                       .then_inc(o_evac, 1)

            act.wait_ge(rope_angle, 2)
            act.activation(sint[:, :, :], ang[:, :, :], ACT.Sin).then_inc(rope_done, 1)
            act.activation(cost[:, :, :], angc[:, :, :], ACT.Sin).then_inc(rope_done, 1)
            act.wait_ge(x_in, 48)
            with act.Fori(0, DEPTH) as l:
                sums("mix")
                act.wait_ge(s5_in, N_S5_IN)
                act.activation(s5v[:, 0, :], sa[:, 2, :], ACT.Exp).then_inc(s5_dt, 1)
                act.wait_ge(s5_ang, 1)
                act.activation(s5v[:, 4, :], s5v[:, 1, :], ACT.Exp).then_inc(s5_trig, 1)
                act.wait_ge(s5_ang, 3)
                act.activation(s5v[:, 5, :], s5v[:, 2, :], ACT.Sin).then_inc(s5_trig, 1)
                act.activation(s5v[:, 6, :], s5v[:, 3, :], ACT.Sin).then_inc(s5_trig, 1)
                act.wait_ge(norm["mix", "tr"], 8)
                for g in GROUPS:
                    if g == ("z", 0):
                        for k in range(2):
                            act.wait_ge(ypre_ready, k + 1)
                            act.activation(gT[:, k, :], gT[:, k, :], ACT.Gelu_apprx_tanh).then_inc(gelu_done, 1)
                    evac(g)
                    if g == ("gate", 3):
                        act.wait_ge(qk_mean, 1)
                        act.activation(qstat[:, 2, :], qstat[:, 1, :], ACT.Sqrt).then_inc(qk_root, 1)
                exps(0)
                for n in range(len(UNITS)):
                    if n + 1 < len(UNITS):
                        exps(n + 1)
                    evac_probs(n)
                sums("ffn")
                for i in range(2):
                    act.wait_ge(r_exp_in, i + 1)
                    if i == 0:
                        act.activation(rt[:, 7, :, 0:4], rt[:, 6, :, 0:4], ACT.Exp).then_inc(r_exp, 1)
                    else:
                        act.activation(rs[:, 7, :], rs[:, 6, :], ACT.Exp).then_inc(r_exp, 1)
                act.wait_ge(rounds_ready, 1)
                nb = act.value_load(rounds[0:1, 0:1], min_val=1, max_val=S // CAP)
                with act.Fori(0, nb) as b:
                    with act.Fori(0, PAIRS) as p:
                        it = b * PAIRS + p
                        wait_reg(act, swt_tr, it + 1)
                        act.activation(selwT, bank[:, 4, :], ACT.Copy).then_inc(swt_ready, 1)
                        for e in range(2):
                            wait_reg(act, up_free[e], it + 2)
                            act.activation(silu[e].rearrange("p a b -> p (a b)"), bank[:, 2 + e, 0:KF * CAP],
                                           ACT.Silu).then_inc(silu_done, 1)
                        wait_reg(act, down_free[1], it + 2)
                        act.activation(yslot[:, 0:512], bank[:, 4, :], ACT.Copy)
                        act.activation(yslot[:, 512:1024], bank[:, 5, :], ACT.Copy).then_inc(y_ready, 1)
                close_layer(act, l)

        @block.vector
        def _(dve):
            TT, TS, STT = dve.tensor_tensor, dve.tensor_scalar, dve.scalar_tensor_tensor

            def bc(ap, n):
                shape = list(ap.shape)
                return ap.unsqueeze(len(shape)).broadcast_to(shape + [n])

            def mid(ap, n):
                p, m = ap.shape
                return ap.unsqueeze(1).broadcast_to([p, n, m])

            def reduce_angle(link, src, k, sin_in, cos_in, last):
                link.do(TS(k, src, 1.0 / TWO_PI, ROUND, ALU.mult, ALU.add))
                link.do(TS(k, k, ROUND, None, ALU.subtract))
                link.do(STT(sin_in, k, -PI_1, src, ALU.mult, ALU.add))
                link.do(STT(sin_in, k, -PI_2, sin_in, ALU.mult, ALU.add))
                link.do(STT(sin_in, k, -PI_3, sin_in, ALU.mult, ALU.add))
                link.do(TS(cos_in, sin_in, np.pi / 2, None, ALU.add))
                link.do(TS(k, cos_in, float(np.pi), TWO_PI, ALU.is_gt, ALU.mult))
                link.do(TT(cos_in, cos_in, k, ALU.subtract))
                TS(cos_in, cos_in, PI_MAX, -PI_MAX, ALU.min, ALU.max).then_inc(last, 1)
                TS(sin_in, sin_in, PI_MAX, -PI_MAX, ALU.min, ALU.max).then_inc(last, 1)

            for tile in (scm[:, :, :, :], bbw[:, :, :, :], scanbuf):
                dve.memset(tile, 0.0).then_inc(dve_const, 1)
            dve.memset(pos_i[:, :], 0).then_inc(dve_const, 1)
            inv = (np.float32(500000.0) ** (-np.arange(0, 16, 2, dtype=np.float32) / np.float32(16)))
            for i in range(HALF):
                m = dve.memset(invf[:, i:i + 1], float(inv[i]))
            m.then_inc(dve_const, 1)
            for i in range(NE):
                m = dve.memset(desc[:, i:i + 1], float(NE - i))
            m.then_inc(dve_const, 1)
            for i in range(8):
                m = dve.memset(thr[:, i:i + 1], float(CAP * (i + 1)))
            m.then_inc(dve_const, 1)
            dve.memset(k2, 0.0).then_inc(dve_const, 1)
            dve.wait_ge(pool_const, N_POOL)
            dve.tensor_copy(iota[:, :], iota_i[:, :]).then_inc(dve_const, 1)
            dve.wait_ge(dve_const, N_DVE_CONST)
            dve.wait_ge(x_in, 48)
            link0 = Chain(dve, sem("rope_chain", False))
            link0.do(dve.tensor_copy(posf[:, :], pos_i[:, :]))
            link0.do(TT(ang[:, :, :], bc(posf[:, :], HALF), mid(invf[:, :], 5), ALU.mult))
            link0.do(dve.tensor_copy(cost[:, :, :], ang[:, :, :]))
            reduce_angle(link0, cost[:, :, :], angk[:, :, :], ang[:, :, :], angc[:, :, :], rope_angle)
            dve.wait_ge(rope_done, 2)

            with dve.Fori(0, DEPTH) as l:
                link = Chain(dve, dve_chain)
                do = link.do

                def normalise(which, gain):
                    dve.wait_ge(norm[which, "sums"], NT)
                    TS(stat[:, 1, :], stat[:, 0, :], 1.0 / D, EPS, ALU.mult, ALU.add).then_inc(norm[which, "mean"], 1)
                    dve.wait_ge(norm[which, "root"], 1)
                    do(dve.reciprocal(stat[:, 0, :], stat[:, 2, :]))
                    for t in range(NT):
                        TS(h[:, t, :], x[:, t, :], stat[:, 0, t:t + 1], None, ALU.mult).then_inc(norm[which, "h"], 1)
                    dve.wait_ge(mix_in, N_MIX_IN)
                    for i in range(2 * NT):
                        t, q = i // 2, i % 2
                        dve.wait_ge(norm[which, "tr"], i + 1)
                        TT(hT[:, 4 * q:4 * q + 4, P * t:P * t + P], bank[:, i % 4, :].rearrange("p (k t) -> p k t", k=4),
                           bc(gain[:, 4 * q:4 * q + 4], P), ALU.mult).then_inc(norm[which, "hT"], 1)

                normalise("mix", g_mix)

                v = lambda i: s5v[:, i, :]
                DT, LD, SIN, COSI, MAG, SN, CS, LRE, T0, T1, T2, DEN, FRE, FIM, ANG, KK = range(16)
                dve.wait_ge(s5_in, N_S5_IN)
                do(TS(v(LRE), sa[:, 0, :], -1e-4, None, ALU.min))
                dve.wait_ge(s5_dt, 1)
                TT(v(LD), v(LRE), v(DT), ALU.mult).then_inc(s5_ang, 1)
                do(TT(v(ANG), sa[:, 1, :], v(DT), ALU.mult))
                reduce_angle(link, v(ANG), v(KK), v(SIN), v(COSI), s5_ang)
                dve.wait_ge(s5_trig, 3)
                pre, pim, nim = (lambda k: pw[:, k, 0, :]), (lambda k: pw[:, k, 1, :]), (lambda k: pw[:, k, 2, :])
                do(TT(pre(0), v(MAG), v(CS), ALU.mult))
                do(TT(pim(0), v(MAG), v(SN), ALU.mult))
                do(TT(v(T0), v(LRE), v(LRE), ALU.mult))
                do(TT(v(T1), sa[:, 1, :], sa[:, 1, :], ALU.mult))
                do(TT(v(DEN), v(T0), v(T1), ALU.add))
                do(dve.reciprocal(v(DEN), v(DEN)))
                do(TS(v(T2), pre(0), 1.0, None, ALU.subtract))
                do(TT(v(T0), v(T2), v(LRE), ALU.mult))
                do(TT(v(T1), pim(0), sa[:, 1, :], ALU.mult))
                do(TT(v(T0), v(T0), v(T1), ALU.add))
                do(TT(v(FRE), v(T0), v(DEN), ALU.mult))
                do(TT(v(T0), pim(0), v(LRE), ALU.mult))
                do(TT(v(T1), v(T2), sa[:, 1, :], ALU.mult))
                do(TT(v(T0), v(T0), v(T1), ALU.subtract))
                do(TT(v(FIM), v(T0), v(DEN), ALU.mult))
                for i, (f, m) in enumerate(((FRE, 0), (FIM, 1), (FRE, 1), (FIM, 0))):
                    do(TT(bbt[:, i, :, :], bc(v(f), SCH), sbm[:, m, :, :], ALU.mult))
                for i, op in ((0, ALU.subtract), (1, ALU.add)):
                    for g in range(2):
                        rows = slice(DH * g, DH * g + DH)
                        TT(bbw[rows, i, :, SCH * g:SCH * g + SCH], bbt[rows, 2 * i, :, :], bbt[rows, 2 * i + 1, :, :],
                           op).then_inc(bb_ready, 1)
                for k in range(9):
                    do(TS(nim(k), pim(k), -1.0, None, ALU.mult))
                    if k < 8:
                        do(TT(v(T0), pre(k), pre(k), ALU.mult))
                        do(TT(v(T1), pim(k), pim(k), ALU.mult))
                        do(TT(pre(k + 1), v(T0), v(T1), ALU.subtract))
                        do(TT(v(T2), pre(k), pim(k), ALU.mult))
                        do(TS(pim(k + 1), v(T2), 2.0, None, ALU.mult))
                dve.wait_ge(s5_tr, 1)
                dve.tensor_copy(bT[:, :, :, :].rearrange("p a b c -> p (a b c)"), bank[:, 4, :]).then_inc(s5_mat, 1)
                dve.tensor_copy(cT[:, 0, :, :].rearrange("p b c -> p (b c)"), bank[:, 5, 0:2 * P]).then_inc(s5_mat, 1)
                TS(cT[:, 1, :, :].rearrange("p b c -> p (b c)"), bank[:, 5, 2 * P:4 * P], -1.0, None, ALU.mult)\
                    .then_inc(s5_mat, 1)

                def scan(T):
                    A = [scanbuf[:, 0, :], scanbuf[:, 1, :]]
                    B = [scanbuf[:, 2, :], scanbuf[:, 3, :]]
                    if T:
                        dve.wait_ge(scan_done, T)
                    dve.wait_ge(bu_done, T + 1)
                    for i in range(2):
                        r = dve.tensor_copy(A[i][:, PAD:PAD + S], bank[:, 4 + i, :])
                        if i == 0:
                            last = [link(r), 0]
                        else:
                            r.then_inc(bu_copied, 1)
                    for k in range(9):
                        sh = 1 << k
                        src = A if k % 2 == 0 else B
                        ar, ai, ni = (pw[:, k, i, T:T + 1] for i in range(3))
                        cur = [s[:, PAD:PAD + S] for s in src]
                        old = [s[:, PAD - sh:PAD + S - sh] for s in src]
                        if k == 8:
                            dst = [s5out[:, T % 2, i, :] for i in range(2)]
                            if T >= 2:
                                dve.wait_ge(y_done, T - 1)
                        else:
                            dst = [s[:, PAD:PAD + S] for s in (B if k % 2 == 0 else A)]
                        if k == 0:
                            dve.wait_ge(bu_copied, T + 1)
                        else:
                            link.sync(last[1])
                        n0 = link(STT(dst[0], old[0], ar, cur[0], ALU.mult, ALU.add))
                        n1 = link(STT(dst[1], old[1], ar, cur[1], ALU.mult, ALU.add))
                        link.sync(n0)
                        r = STT(dst[0], old[1], ni, dst[0], ALU.mult, ALU.add)
                        last[0] = link(r)
                        link.sync(n1)
                        r = STT(dst[1], old[0], ai, dst[1], ALU.mult, ALU.add)
                        if k == 8:
                            r.then_inc(scan_done, 1)
                        else:
                            last[1] = link(r)

                def sums_qk():
                    dve.wait_ge(pj_evac, GIDX[("ng", 0)] + 1)
                    for t in range(NT):
                        do(TT(sq[:, :], raw[:, t, :], raw[:, t, :], ALU.mult))
                        do(dve.tensor_reduce(qstat[:, 0, 16 * t:16 * t + 16],
                                             sq[:, :].rearrange("p (n d) -> p n d", d=DH), AX.X, ALU.add))
                    do(TT(sq[0:NCMP, 0:P], kcraw[0:NCMP, :], kcraw[0:NCMP, :], ALU.mult))
                    do(dve.tensor_reduce(qstat[0:NCMP, 0, 64:66],
                                         sq[0:NCMP, 0:P].rearrange("p (n d) -> p n d", d=DH), AX.X, ALU.add))
                    TS(qstat[:, 1, :], qstat[:, 0, :], 1.0 / DH, EPS, ALU.mult, ALU.add).then_inc(qk_mean, 1)

                def rope(X, n, rows, col):
                    x1, x2 = X[:, :, 0:HALF], X[:, :, HALF:2 * HALF]
                    c, s = mid(cost[rows, col, :], n), mid(sint[rows, col, :], n)
                    for i, (u, w) in enumerate(((x1, c), (x2, s), (x2, c), (x1, s))):
                        link(TT(rtmp[rows, i, 0:n, :], u, w, ALU.mult))
                    link.sync()
                    r1 = TT(x1, rtmp[rows, 0, 0:n, :], rtmp[rows, 1, 0:n, :], ALU.subtract)
                    r2 = TT(x2, rtmp[rows, 2, 0:n, :], rtmp[rows, 3, 0:n, :], ALU.add)
                    return r1, r2

                def norm_qk(t):
                    if t >= 2:
                        dve.wait_ge(pj_done, GIDX[("tk", t - 2)] + 1)
                    r = qstat[:, 0, 16 * t:16 * t + 16]
                    Q = qn[:, t % 2, 0:512]
                    K = qn[:, t % 2, 512:768]
                    for hh in range(2):
                        link(TT(Q.rearrange("p (g h d) -> p h g d", g=GRP, h=2)[:, hh], 
                                raw[:, t, 256 * hh:256 * hh + 256].rearrange("p (g d) -> p g d", d=DH),
                                bc(r[:, 4 * hh:4 * hh + 4], DH), ALU.mult))
                        link(TT(K[:, P * hh:P * hh + P].rearrange("p (g d) -> p g d", d=DH),
                                raw[:, t, 512 + 256 * hh:640 + 256 * hh].rearrange("p (g d) -> p g d", d=DH),
                                bc(r[:, 8 + 4 * hh:10 + 4 * hh], DH), ALU.mult))
                    link.sync()
                    Q3 = Q.rearrange("p (g d) -> p g d", d=DH)
                    K3 = K.rearrange("p (g d) -> p g d", d=DH)
                    link(TT(Q3, Q3, mid(q_gain[:, :], 8), ALU.mult))
                    do(TT(K3, K3, mid(k_gain[:, :], 4), ALU.mult))
                    r1, r2 = rope(qn[:, t % 2, :].rearrange("p (g d) -> p g d", d=DH), 12, slice(0, P), t)
                    link(r1)
                    r2.then_inc(qk_ready, 1)

                for T in range(4):
                    scan(T)
                sums_qk()
                for T in range(4, NST):
                    scan(T)
                for k in range(2):
                    dve.wait_ge(y_done, 4 * k + 4)
                    STT(gT[:, k, :], uT[:, k, :], sd[:, k:k + 1], bank[:, 6 + k, :], ALU.mult, ALU.add)\
                        .then_inc(ypre_ready, 1)
                dve.wait_ge(qk_root, 1)
                do(dve.reciprocal(qstat[:, 0, :], qstat[:, 2, :]))
                for t in range(NT):
                    norm_qk(t)
                K3 = kcn[0:NCMP, :].rearrange("p (g d) -> p g d", d=DH)
                do(TT(K3, kcraw[0:NCMP, :].rearrange("p (g d) -> p g d", d=DH), bc(qstat[0:NCMP, 0, 64:66], DH), ALU.mult))
                do(TT(K3, K3, mid(k_gain[0:NCMP, :], 2), ALU.mult))
                r1, r2 = rope(K3, 2, slice(0, NCMP), NT)
                link(r1)
                r2.then_inc(kcn_ready, 1)
                dve.wait_ge(pj_evac, GIDX[("z", 3)] + 1)
                for m in range(2):
                    TT(sT[:, m, :], zval[:, m, :], zsig[:, m, :], ALU.mult).then_inc(sT_ready, 1)

                def maxima(n):
                    qt, j, br = UNITS[n]
                    nk = NCMP if br == CMPB else P * (qt + 1)
                    for g in range(GRP):
                        dve.wait_ge(score_done, GRP * n + g + 1)
                        do(dve.tensor_reduce(nmax[:, n % 2, g:g + 1], bank[:, g, 0:nk], AX.X, ALU.max))
                        TS(nbias[:, n % 2, g:g + 1], nmax[:, n % 2, g:g + 1], -SCALE, None, ALU.mult)\
                            .then_inc(max_ready, 1)

                def weigh(n):
                    qt, j, br = UNITS[n]
                    nk = NCMP if br == CMPB else P * (qt + 1)
                    s = rscale[:, n % 2, :]
                    dve.wait_ge(exp_done, GRP * n + GRP)
                    do(dve.reciprocal(s, rsum[:, n % 2, :]))
                    gv = gsig[:, qt, 3 * GRP * j + br:3 * GRP * j + br + 3 * (GRP - 1) + 1:3]
                    do(TT(s, s, gv, ALU.mult))
                    if br == CMPB and qt == 0:
                        do(TS(s, s, some[:, 0:1], None, ALU.mult))
                    for g in range(GRP):
                        pr = prob[:, n % 2, g, 0:nk]
                        TS(pr, pr, s[:, g:g + 1], None, ALU.mult).then_inc(p_ready, 1)

                def evac_probs(n):
                    w = NCMP if UNITS[n][2] == CMPB else P
                    for kt in range(key_tiles(UNITS[n])):
                        c = first_tr(n) + kt
                        if c % 2 == 0:
                            continue
                        dve.wait_ge(tr_done, c + 1)
                        if c >= 4:
                            dve.wait_ge(pv_done, c - 3)
                        dve.tensor_copy(pT[0:w, c % 4, :], bank[0:w, 5, :]).then_inc(evac_dve, 1)

                maxima(0)
                for n in range(len(UNITS)):
                    weigh(n)
                    if n + 1 < len(UNITS):
                        maxima(n + 1)
                    evac_probs(n)

                for m in range(KD):
                    dve.wait_ge(merge_mm, m + 1)
                    o = 2 * (m % 2)
                    link(TT(gates[:, m, :], gates[:, m, :], bank[:, o, :], ALU.mult))
                    do(TT(gates[:, 8 + m, :], gates[:, 8 + m, :], bank[:, o + 1, :], ALU.mult))
                    TT(mergedT[:, m, :], gates[:, m, :], gates[:, 8 + m, :], ALU.add).then_inc(merged, 1)
                for i in range(4 * NT):
                    j, t = i // NT, i % NT
                    dve.wait_ge(out_mm, i + 1)
                    xv = x[:, t, CW * j:CW * j + CW]
                    TT(xv, xv, bank[:, 4 + i % 4, 0:CW], ALU.add).then_inc(x_mixed, 1)

                normalise("ffn", g_ffn)
                dve.wait_ge(logit_mm, 1)
                do(TT(lg[:, :, :], bank[:, 4, 0:NT * NR].rearrange("p (t n) -> p t n", n=NR),
                      mid(b_r[:, :], NT), ALU.add))
                R = lambda i, n=NE: rt[:, i, :, 0:n]
                V = lambda i: rs[:, i, :]

                def first_max(src, n, hot, top):
                    do(dve.tensor_reduce(top, src, AX.X, ALU.max))
                    do(TT(hot, src, bc(top, n), ALU.is_equal))
                    do(TT(hot, hot, mid(desc[:, 0:n], NT), ALU.mult))
                    do(dve.tensor_reduce(V(11), hot, AX.X, ALU.max))
                    do(TT(hot, mid(desc[:, 0:n], NT), bc(V(11), n), ALU.is_equal))

                gl = lg[:, :, 0:4]
                first_max(gl, 4, R(0, 4), V(0))
                TT(R(6, 4), gl, bc(V(0), 4), ALU.subtract).then_inc(r_exp_in, 1)
                dve.wait_ge(r_exp, 1)
                do(dve.tensor_reduce(V(1), R(7, 4), AX.X, ALU.add))
                do(dve.reciprocal(V(1), V(1)))
                g4 = lambda ap: ap.rearrange("p t (g e) -> p t g e", g=4)
                do(TS(R(1, 4), R(0, 4), BIG, -BIG, ALU.mult, ALU.add))
                for t in range(NT):
                    link(TT(g4(R(2))[:, t], g4(lg[:, :, 4:NR])[:, t], bc(rt[:, 0, t, 0:4], 8), ALU.mult))
                link.sync()
                for t in range(NT):
                    link(TT(g4(R(2))[:, t], g4(R(2))[:, t], bc(rt[:, 1, t, 0:4], 8), ALU.add))
                link.sync()
                first_max(R(2), NE, R(3), V(2))
                do(TS(R(4), R(3), -3 * BIG, None, ALU.mult))
                do(TT(R(2), R(2), R(4), ALU.add))
                first_max(R(2), NE, R(4), V(3))
                TT(V(6), V(3), V(2), ALU.subtract).then_inc(r_exp_in, 1)
                dve.wait_ge(r_exp, 2)
                do(TS(V(4), V(7), 1.0, None, ALU.add))
                do(dve.reciprocal(V(4), V(4)))
                do(TT(V(4), V(4), V(1), ALU.mult))
                do(TT(V(5), V(4), V(7), ALU.mult))
                TT(member[:, :, :], R(3), R(4), ALU.add).then_inc(r_member, 1)
                do(TT(R(5), R(3), bc(V(4), NE), ALU.mult))
                do(TT(R(1), R(4), bc(V(5), NE), ALU.mult))
                TT(wmem[:, :, :], R(5), R(1), ALU.add).then_inc(r_member, 1)
                dve.wait_ge(r_member, 2)
                dve.wait_ge(prefix_mm, 1)
                do(STT(slot[:, :, :], bank[:, 5, 0:NT * NE].rearrange("p (t n) -> p t n", n=NE), 1.0, member[:, :, :],
                       ALU.add, ALU.mult))
                do(TS(slot[:, :, :], slot[:, :, :], 1.0, None, ALU.subtract))
                do(dve.tensor_reduce(cnt[:, 8:9], bank[:, 5, NT * NE:NT * NE + NE], AX.X, ALU.max))
                do(TS(cnt[:, 0:8], thr[:, :], cnt[:, 8:9], None, ALU.is_lt))
                do(dve.tensor_reduce(cnt[:, 9:10], cnt[:, 0:8], AX.X, ALU.add))
                do(TS(cnt[:, 9:10], cnt[:, 9:10], 1.0, None, ALU.add))
                dve.memset(yslot, 0.0).then_inc(y_ready, 1)
                dve.memset(selwT, 0.0).then_inc(swt_ready, 1)
                dve.sem_inc(put_add, 2)
                dve.tensor_copy(rounds[:, :], cnt[:, 9:10]).then_inc(rounds_ready, 1)
                dve.wait_ge(rounds_ready, 1)
                nb = dve.value_load(rounds[0:1, 0:1], min_val=1, max_val=S // CAP)

                def add_put(base):
                    for s in range(2 * NT):
                        t, half = s // 2, s % 2
                        wait_reg(dve, put_mm, base + (s + 1))
                        xv = x[:, t, 512 * half:512 * half + 512]
                        TT(xv, xv, bank[:, 6 + s % 2, :], ALU.add).then_inc(put_add, 1)

                with dve.Fori(0, nb) as b:
                    with dve.Fori(0, PAIRS) as p:
                        it = b * PAIRS + p
                        wait_reg(dve, swt_ready, it + 1)
                        dve.tensor_copy(pair[:, 0, :, :], slot[:, :, bass.ds(p * 2, 2)]).then_inc(dve_loop, 1)
                        dve.tensor_copy(pair[:, 1, :, :], wmem[:, :, bass.ds(p * 2, 2)]).then_inc(dve_loop, 1)
                        wait_reg(dve, dve_loop, it * 4 + 2)
                        for e in range(2):
                            TT(sel[:, :, e, :], mid(iota[:, :], NT), bc(pair[:, 0, :, e], CAP), ALU.is_equal)\
                                .then_inc(dve_loop, 1)
                        wait_reg(dve, dve_loop, it * 4 + 4)
                        for e in range(2):
                            r = TT(selw[:, :, e, :], sel[:, :, e, :], bc(pair[:, 1, :, e], CAP), ALU.mult)
                        r.then_inc(sel_ready, 1)
                        for e in range(2):
                            wait_reg(dve, xg_done, it * 2 + (e + 1))
                            TT(xg[e], bank[:, e, :].rearrange("p (k c) -> p k c", c=CAP), bc(g_ffn[:, :], CAP), ALU.mult)\
                                .then_inc(xg_ready, 1)
                        add_put(it * 8)
                        for e in range(2):
                            wait_reg(dve, silu_done, it * 2 + (e + 1))
                            TT(actT[e].rearrange("p a b -> p (a b)"), silu[e].rearrange("p a b -> p (a b)"),
                               bank[:, 2 + e, KF * CAP:2 * KF * CAP], ALU.mult).then_inc(act_ready, 1)
                    TS(slot[:, :, :], slot[:, :, :], float(CAP), None, ALU.subtract).then_inc(rounds_ready, 1)
                    wait_reg(dve, rounds_ready, b + 2)
                add_put(nb * (PAIRS * 8))
                close_layer(dve, l)


_INS = ['x', 'positions', 'norm_mix', 'norm_ffn', 'w_in', 'q_gain', 'k_gain', 'cmp_k_pos', 'cmp_k_w1', 'cmp_k_w2',
        'cmp_v_pos', 'cmp_v_w1', 'cmp_v_w2', 's5_a_re', 's5_a_im', 's5_log_dt', 's5_b_re', 's5_b_im', 's5_c_re',
        's5_c_im', 's5_d', 's5_glu', 'proj_nsa', 'proj_s5', 'w_out', 'router_group', 'router_group_bias',
        'router_expert', 'router_expert_bias', 'expert_gate', 'expert_up', 'expert_down']


def kernel(**inputs):
    import numpy as _np
    import concourse.bacc as _bacc
    from concourse import mybir as _mybir
    from concourse.bass_utils import run_bass_kernel_spmd as _run

    nc = _bacc.Bacc("TRN2", target_bir_lowering=False, num_devices=1)
    arrays, aps = {}, {}
    for name in _INS:
        v = _np.ascontiguousarray(inputs[name])
        if name.startswith("expert_"):
            v = v.reshape(v.shape[0] * v.shape[1], v.shape[2], v.shape[3])
        arrays[f"in_{name}"] = v
        aps[name] = nc.dram_tensor(f"in_{name}", v.shape, _mybir.dt.from_np(v.dtype), kind="ExternalInput").ap()
    out = nc.dram_tensor("out_0", (1, 512, 1024), _mybir.dt.float32, kind="ExternalOutput").ap()
    trunk(nc, aps, out)
    r = _run(nc, [arrays], core_ids=[0])
    return r.results[0]["out_0"]
```

```python
from contextlib import ExitStack

import numpy as np

import concourse.bass as bass
from concourse import mybir

F32 = mybir.dt.float32
I32 = mybir.dt.int32
ALU = mybir.AluOpType
ACT = mybir.ActivationFunctionType
AX = mybir.AxisListType

P = 128
D = 1024
S = 512
NT = S // P
KD = D // P
DEPTH = 2
HEADS = 8
KVH = 2
GRP = HEADS // KVH
DH = 64
HALF = 8
NCMP = 31
CSTR = 16
CBLK = 32
NST = 8
SCH = 16
NE = 32
FF = 512
KF = FF // P
CAP = 64
PAIRS = NE // 2
NR = 4 + NE
EPS = 1e-6
BIG = 1e30
SCALE = DH ** -0.5
C_Q, C_KC, C_KS, C_G, C_U, C_GA, C_GS = 0, 512, 768, 1280, 1304, 1560, 2584
CW = 256
TWO_PI = 2 * np.pi
PI_1 = 6.28125
PI_2 = float(np.float32(np.float64(int((TWO_PI - PI_1) * 2 ** 21)) / 2 ** 21))
PI_3 = float(np.float32(TWO_PI - PI_1 - PI_2))
PI_MAX = 3.1415925
ROUND = 12582912.0

CHUNKS = ([("w_in", C_U, KD, CW), ("w_in", C_KC, KD, CW), ("w_in", C_Q, KD, CW), ("w_in", C_Q + CW, KD, CW),
           ("w_in", C_KS, KD, CW), ("w_in", C_KS + CW, KD, CW)]
          + [("w_in", C_GA + CW * j, KD, CW) for j in range(8)]
          + [("proj_s5", 0, 2, D), ("proj_nsa", 0, 4, 512), ("proj_nsa", 512, 4, 512)]
          + [("w_out", CW * j, KD, CW) for j in range(4)])
NRING = 3

SEQ = [("u", 0), ("u", 1), ("s5t", 0), ("bu", 0), ("kc", 0), ("vc", 0), ("bu", 1), ("hid", 0), ("hid", 1)]
SEQ += [("tok", 2, t) for t in range(NT)] + [("y", 0), ("bu", 2)]
SEQ += [("tok", 3, t) for t in range(NT)] + [("cmp", 0), ("cmp", 1), ("y", 1), ("bu", 3)]
SEQ += [("tok", 4, t) for t in range(NT)] + [("y", 2), ("bu", 4)]
SEQ += [("tok", 5, t) for t in range(NT)] + [("ng", 0), ("y", 3), ("bu", 5)]
SEQ += [("gate", 0), ("gate", 1), ("gate", 2), ("y", 4), ("bu", 6), ("gate", 3), ("gate", 4), ("gate", 5), ("y", 5), ("bu", 7)]
SEQ += [("gate", 6), ("gate", 7), ("gate", 8), ("y", 6), ("gate", 9), ("gate", 10), ("gate", 11), ("y", 7)]
SEQ += [("gate", i) for i in range(12, 16)] + [("z", m) for m in range(4)]
SEQ += [x for t in range(NT) for x in (("tq", t), ("tk", t))] + [("tkc", 0)]
GROUPS = [s for s in SEQ if s[0] not in ("s5t", "bu", "y")]
GIDX = {g: i for i, g in enumerate(GROUPS)}
NBANK = 4

CMPB, SLC, WIN = range(3)
UNITS = [(qt, j, br) for qt in range(NT) for j in range(KVH) for br in range(3)]


def key_tiles(unit):
    qt, j, br = unit
    return 1 if br == CMPB else qt + 1


def first_tr(n):
    return sum(key_tiles(u) for u in UNITS[:n])


def trunk(nc, a, out):
    with ExitStack() as ctx:
        def sb(name, shape, dt=F32):
            return ctx.enter_context(nc.sbuf_tensor(name, shape, dt))

        sems = []

        def sem(name, layer=True):
            s = ctx.enter_context(nc.semaphore(name))
            if layer:
                sems.append(s)
            return s

        x = sb("x", [P, NT, D])
        h = sb("h", [P, NT, D])
        hT = sb("hT", [P, KD, S])
        raw = h
        mergedT = hT
        gate_a = sb("gate_a", [P, KD, FF])
        KB = 256
        arena = sb("arena", [P, 130 * KB])

        def view(at_kb, *shape):
            n = int(np.prod(shape))
            v = arena[:, int(at_kb * KB):int(at_kb * KB) + n]
            names = "abcd"[:len(shape)]
            if len(shape) == 1:
                return v
            return v.rearrange(f"p ({' '.join(names)}) -> p {' '.join(names)}", **dict(zip(names, shape)))

        gate_w = [gate_a[:, :, :], view(0, KD, FF)]
        up_w = [view(16, KD, FF), view(32, KD, FF)]
        down_w = [view(48, KF, D), view(64, KF, D)]
        xrow = view(80, D)
        xg = view(88, KD, 2 * CAP)
        hid = view(97, FF)
        actT = [view(84, KF, CAP), view(85, KF, CAP)]
        silu = view(86, FF)
        yslot = view(92, D)
        ytok = [view(4 * i, D) for i in range(2 * NT)]
        ring = [view(8 * i, KD * CW) for i in range(NRING)]
        gates = view(24, 16, S)
        qn = view(56, 2, 12 * DH)
        qT = view(62, GRP, S)
        kT = view(70, 2, S)
        k2 = view(74, 4, S)
        w1 = view(82, 2, 16, P)
        prob = view(74, 2, GRP, S)
        pT = view(90, 4, S)
        zval = view(74, 2, S)
        zsig = view(78, 2, S)
        oT = view(98, GRP, S)
        s5out = view(98, 2, 2, S)
        uT = view(110, 2, S)
        sT = uT
        kcraw, kcn, vcs = (view(106 + i / 2, P) for i in range(3))
        gcmp = view(107.5, 2, 64)
        PAD = 256
        scanbuf = view(114, 4, PAD + S)
        gT = view(126, 2, S)
        junk = view(126, D)

        spare = gate_a[:, :, :].rearrange("p k n -> p (k n)")
        sq = spare[:, 0:D]
        w_glu = spare[:, D:2 * D].rearrange("p (k n) -> p k n", k=2)
        bbt = spare[:, 2 * D:2 * D + 512].rearrange("p (i t c) -> p i t c", i=4, t=NST)
        sbm = spare[:, 2 * D + 512:2 * D + 768].rearrange("p (i t c) -> p i t c", i=2, t=NST)
        bT, cT = (spare[:, 2 * D + 768 + 512 * i:2 * D + 1280 + 512 * i].rearrange("p (i k n) -> p i k n", i=2, k=2)
                  for i in range(2))
        rtmp = spare[:, 2 * D:2 * D + 384].rearrange("p (i g d) -> p i g d", i=4, g=12)
        gsig = spare[:, 3840:3840 + 24 * NT].rearrange("p (t n) -> p t n", t=NT)
        w_ng = view(108, KD, 24)
        w2 = view(109, 2, DH)
        rt = view(100, 8, NT, NE)
        member = view(104, NT, NE)
        lg = view(106, NT, NR)
        ident = sb("ident", [P, P])
        causal = sb("causal", [P, P])
        before = sb("before", [P, P])
        ones = sb("ones", [P, P])
        cmpmask = sb("cmpmask", [P, NT, NCMP + 1])
        some = sb("some", [P, 1])
        tok_i = sb("tok_i", [P, NT], I32)
        eid = sb("eid", [P, NE])
        desc = sb("desc", [P, NE])
        thr = sb("thr", [P, 8])
        invf = sb("invf", [P, HALF])
        pos_i = sb("pos_i", [P, 5], I32)
        posf = sb("posf", [P, 5])
        ang = sb("ang", [P, 5, HALF])
        angk = sb("angk", [P, 5, HALF])
        angc = sb("angc", [P, 5, HALF])
        cost = sb("cost", [P, 5, HALF])
        sint = sb("sint", [P, 5, HALF])
        g_mix = sb("g_mix", [P, KD])
        g_ffn = sb("g_ffn", [P, KD])
        q_gain = sb("q_gain", [P, DH])
        k_gain = sb("k_gain", [P, DH])
        cpos = sb("cpos", [P, 2, CSTR])
        w_r = sb("w_r", [P, KD, NR])
        b_r = sb("b_r", [P, NR])
        sa = sb("sa", [P, 3, NST])
        scm = sb("scm", [P, 2, 2, P])
        sd = sb("sd", [P, 2])
        s5v = sb("s5v", [P, 24, NST])
        pw = sb("pw", [P, 9, 3, NST])
        bbw = sb("bbw", [P, 2, NST, 2 * SCH])
        stat = sb("stat", [P, 3, 4])
        qstat = sb("qstat", [P, 3, 66])
        hb = sb("hb", [P, 2])
        kcT = sb("kcT", [P, NCMP + 1])
        nmax = sb("nmax", [P, 2, GRP])
        nbias = sb("nbias", [P, 2, GRP])
        rsum = sb("rsum", [P, 2, GRP])
        rscale = sb("rscale", [P, 2, GRP])
        rs = sb("rs", [P, 12, NT])
        place = sb("place", [P, 8, NT, 2])
        wnow = sb("wnow", [P, NT, 2])
        row_y = sb("row_y", [P, NT, 2], I32)
        row_tab = sb("row_tab", [P, NT, 2], I32)
        table = view(96, P).bitcast(I32)
        slot_tok = view(96.5, 1).bitcast(I32)
        MAXR = S // CAP
        h_rows = nc.dram_tensor("h_rows", (S, D), F32, kind="Internal").ap()
        y_rows = nc.dram_tensor("y_rows", (PAIRS * P, D), F32, kind="Internal").ap()
        tab_rows = nc.dram_tensor("tab_rows", (P * MAXR * PAIRS, 1), I32, kind="Internal").ap()
        cnt = sb("cnt", [P, 10])
        rounds = sb("rounds", [P, 1], I32)
        bank = ctx.enter_context(nc.psum_tensor("bank", [P, 8, 512], F32))

        x_in = sem("x_in", False)
        pool_const = sem("pool_const", False)
        dve_const = sem("dve_const", False)
        rope_angle = sem("rope_angle", False)
        rope_done = sem("rope_done", False)
        arrived = sem("arrived", False)
        cleared = sem("cleared", False)
        tick = sem("tick", False)
        out_sem = sem("out_sem", False)
        ring_in = [sem(f"ring_in{i}") for i in range(NRING)]
        s5_in = sem("s5_in")
        gain_in = sem("gain_in")
        mix_in = sem("mix_in")
        norm = {}
        for w in ("mix", "ffn"):
            for n in ("sums", "mean", "root", "h", "tr", "hT"):
                norm[w, n] = sem(f"{w}_{n}")
        pj_done = sem("pj_done")
        pj_evac = sem("pj_evac")
        s5_dt = sem("s5_dt")
        s5_ang = sem("s5_ang")
        s5_trig = sem("s5_trig")
        bb_ready = sem("bb_ready")
        s5_tr = sem("s5_tr")
        s5_mat = sem("s5_mat")
        bu_done = sem("bu_done")
        bu_copied = sem("bu_copied")
        scan_done = sem("scan_done")
        y_done = sem("y_done")
        ypre_ready = sem("ypre_ready")
        gelu_done = sem("gelu_done")
        sT_ready = sem("sT_ready")
        qk_mean = sem("qk_mean")
        qk_root = sem("qk_root")
        qk_ready = sem("qk_ready")
        kcn_ready = sem("kcn_ready")
        score_done = sem("score_done")
        max_ready = sem("max_ready")
        exp_done = sem("exp_done")
        p_ready = sem("p_ready")
        tr_done = sem("tr_done")
        evac_act = sem("evac_act")
        evac_dve = sem("evac_dve")
        pv_done = sem("pv_done")
        o_evac = sem("o_evac")
        merge_mm = sem("merge_mm")
        merged = sem("merged")
        out_mm = sem("out_mm")
        x_mixed = sem("x_mixed")
        logit_mm = sem("logit_mm")
        r_exp_in = sem("r_exp_in")
        r_exp = sem("r_exp")
        r_member = sem("r_member")
        prefix_mm = sem("prefix_mm")
        rounds_ready = sem("rounds_ready")
        gate_in = [sem(f"gate_in{i}") for i in range(2)]
        up_in = [sem(f"up_in{i}") for i in range(2)]
        down_in = [sem(f"down_in{i}") for i in range(2)]
        gate_free = [sem(f"gate_free{i}") for i in range(2)]
        up_free = [sem(f"up_free{i}") for i in range(2)]
        down_free = [sem(f"down_free{i}") for i in range(2)]
        table_zero = sem("table_zero")
        table_out = sem("table_out")
        place_ready = sem("place_ready")
        table_put = sem("table_put")
        table_in = sem("table_in")
        h_out = sem("h_out")
        slot_copied = sem("slot_copied")
        rows_in = sem("rows_in")
        xt_done = sem("xt_done")
        xg_ready = sem("xg_ready")
        silu_done = sem("silu_done")
        act_ready = sem("act_ready")
        at_done = sem("at_done")
        at_ready = sem("at_ready")
        y_ready = sem("y_ready")
        y_out = sem("y_out")
        combined = sem("combined")
        w_round = sem("w_round")
        comb_step = sem("comb_step")
        y_tok = [sem(f"y_tok{i}") for i in range(2 * NT)]
        act_chain = sem("act_chain")
        dve_chain = sem("dve_chain")

        N_POOL = 13
        N_DVE_CONST = 9

        def last_use(c):
            if c < 6:
                return pj_done, GIDX[[("u", 1), ("vc", 0)][c] if c < 2 else ("tok", c, NT - 1)] + 1
            if c < 14:
                return pj_done, GIDX[("gate", 2 * (c - 6) + 1)] + 1
            if c < 17:
                return merge_mm, KD // 2 if c == 15 else KD
            return out_mm, NT * (c - 16)

        class Chain:

            def __init__(self, eng, s):
                self.eng, self.s, self.n = eng, s, 0

            def __call__(self, ins):
                ins.then_inc(self.s, 1)
                self.n += 1
                return self.n

            def sync(self, n=None):
                self.eng.wait_ge(self.s, self.n if n is None else n)

            def do(self, ins):
                self(ins)
                self.sync()

        def wait_reg(eng, s, value):
            eng.wait_ge(s, value)
            eng.sem_inc(tick, 1)

        def close_layer(eng, l):
            eng.drain().then_inc(arrived, 1)
            wait_reg(eng, cleared, l + 1)

        def lay(name, l):
            ap = a[name]
            if len(ap.shape) == 2:
                return ap[bass.ds(l, 1), :].rearrange("o n -> (o n)")
            if len(ap.shape) == 3:
                return ap[bass.ds(l, 1), :, :].rearrange("o m n -> (o m) n")
            return ap[bass.ds(l, 1), :, :, :].rearrange("o g m n -> (o g) m n")

        block = ctx.enter_context(nc.Block())

        @block.gpsimd
        def _(pool):
            n = [0]

            def step(ins):
                ins.then_inc(pool_const, 1)
                n[0] += 1

            step(pool.memset(ident[:, :], 0.0))
            step(pool.memset(causal[:, :], 0.0))
            step(pool.memset(before[:, :], 1.0))
            step(pool.memset(cmpmask[:, :, :], 0.0))
            step(pool.memset(some[:, :], 1.0))
            step(pool.iota(tok_i[:, :], [[P, NT]], base=0, channel_multiplier=1))
            pool.wait_ge(pool_const, n[0])
            step(pool.affine_select(out=ident[:, :], in_=ident[:, :], compare_op=ALU.not_equal, fill=1.0,
                                    base=0, pattern=[[-1, P]], channel_multiplier=1))
            step(pool.affine_select(out=causal[:, :], in_=causal[:, :], compare_op=ALU.is_ge, fill=-BIG,
                                    base=0, pattern=[[-1, P]], channel_multiplier=1))
            step(pool.affine_select(out=before[:, :], in_=before[:, :], compare_op=ALU.is_gt, fill=0.0,
                                    base=0, pattern=[[1, P]], channel_multiplier=-1))
            step(pool.affine_select(out=cmpmask[:, :, :], in_=cmpmask[:, :, :], compare_op=ALU.is_ge, fill=-BIG,
                                    base=-(CBLK - 1), pattern=[[P, NT], [-CSTR, NCMP + 1]], channel_multiplier=1))
            step(pool.affine_select(out=some[:, :], in_=some[:, :], compare_op=ALU.is_ge, fill=0.0,
                                    base=-(CBLK - 1), pattern=[[0, 1]], channel_multiplier=1))
            step(pool.memset(ones[:, :], 1.0))
            step(pool.memset(qstat[:, :, :], 1.0))
            assert n[0] == N_POOL
            with pool.Fori(0, DEPTH) as l:
                pool.wait_ge(x_mixed, 4 * NT)
                pool.memset(table, 0).then_inc(table_zero, 1)
                pool.wait_ge(table_zero, 1)
                pool.dma_start(tab_rows.rearrange("(p n) o -> p (n o)", p=P), table).then_inc(table_out, 16)
                pool.wait_ge(table_out, 16)
                pool.wait_ge(place_ready, 2)
                for t in range(NT):
                    for k in range(2):
                        pool.indirect_dma_start(tab_rows[:, :], bass.IndirectOffsetOnAxis(ap=row_tab[:, t, k:k + 1], axis=0),
                                                tok_i[:, t:t + 1], None).then_inc(table_put, 16)
                pool.wait_ge(table_put, 16 * 2 * NT)
                pool.dma_start(table, tab_rows.rearrange("(p n) o -> p (n o)", p=P)).then_inc(table_in, 16)
                pool.wait_ge(table_in, 16)
                pool.wait_ge(h_out, 16)
                pool.wait_ge(rounds_ready, 1)
                nb = pool.value_load(rounds[0:1, 0:1], min_val=1, max_val=MAXR)
                with pool.Fori(0, nb) as b:
                    with pool.Fori(0, PAIRS) as p:
                        it = b * PAIRS + p
                        wait_reg(pool, xg_ready, it * 2 + 1)
                        pool.tensor_copy(slot_tok, table[:, bass.ds(it, 1)]).then_inc(slot_copied, 1)
                        wait_reg(pool, slot_copied, it + 1)
                        pool.indirect_dma_start(xrow, None, h_rows[:, :],
                                                bass.IndirectOffsetOnAxis(ap=slot_tok, axis=0)).then_inc(rows_in, 16)
                    wait_reg(pool, y_out, b * (PAIRS * 16) + (PAIRS * 16 + 16))
                    for k in range(2):
                        for t in range(NT):
                            pool.indirect_dma_start(ytok[2 * t + k], None, y_rows[:, :],
                                                    bass.IndirectOffsetOnAxis(ap=row_y[:, t, k:k + 1], axis=0))\
                                .then_inc(y_tok[2 * t + k], 16)
                    wait_reg(pool, combined, b + 2)
                pool.dma_reset()
                wait_reg(pool, arrived, (l + 1) * 4)
                for s in sems:
                    pool.sem_clear(s)
                pool.sem_inc(cleared, 1)

        @block.sync
        def _(sp):
            sp.dma_start(x[:, :, :], a["x"][0].rearrange("(t p) d -> p t d", p=P)).then_inc(x_in, 16)
            sp.wait_ge(dve_const, N_DVE_CONST)
            sp.dma_start(pos_i[:, 0:NT], a["positions"][0].rearrange("(t p) -> p t", p=P),
                         allow_slow_non_contiguous=True).then_inc(x_in, 16)
            sp.dma_start(pos_i[0:NCMP, NT:NT + 1],
                         a["positions"][0, CBLK - 1:S].rearrange("(c o) -> c o", o=1)[0:(NCMP - 1) * CSTR + 1:CSTR, :],
                         allow_slow_non_contiguous=True).then_inc(x_in, 16)
            with sp.Fori(0, DEPTH) as l:
                def small(s, dst, src):
                    sp.dma_start(dst, src, allow_slow_non_contiguous=True).then_inc(s, 16)

                def weights(c):
                    name, col, k, n = CHUNKS[c]
                    if c >= NRING:
                        sp.wait_ge(*last_use(c - NRING))
                    dst = ring[c % NRING].rearrange("p (k n) -> p k n", k=k)
                    if name == "proj_nsa":
                        src = lay(name, l)[:, col:col + n].rearrange("(j g d) n -> j d g n", j=KVH, g=GRP)
                        for j in range(KVH):
                            for g in range(GRP):
                                sp.dma_start(dst[DH * j:DH * j + DH, g, :], src[j, :, g, :]).then_inc(ring_in[c % NRING], 16)
                    else:
                        src = lay(name, l)[:, col:col + n].rearrange("(k p) n -> p k n", p=P)
                        sp.dma_start(dst, src).then_inc(ring_in[c % NRING], 16)

                small(gain_in, g_mix[:, :], lay("norm_mix", l).rearrange("(k p) -> p k", p=P))
                small(gain_in, g_ffn[:, :], lay("norm_ffn", l).rearrange("(k p) -> p k", p=P))
                weights(0)
                for i, name in enumerate(("s5_a_re", "s5_a_im")):
                    small(s5_in, sa[:, i, :], lay(name, l).rearrange("(t g) n -> (g n) t", g=2))
                dts = lay("s5_log_dt", l).rearrange("(t g) -> g t", g=2)
                for g in range(2):
                    small(s5_in, sa[DH * g:DH * g + DH, 2, :], dts[g:g + 1, :].broadcast_to([DH, NST]))
                for i, name in enumerate(("s5_b_re", "s5_b_im")):
                    small(s5_in, sbm[:, i, :, :], lay(name, l).rearrange("(t g) n c -> (g n) t c", g=2))
                for i, name in enumerate(("s5_c_re", "s5_c_im")):
                    cv = lay(name, l).rearrange("(k j g) c n -> k j g c n", k=2, g=2)
                    for k in range(2):
                        for j in range(4):
                            for g in range(2):
                                r = 32 * j + SCH * g
                                small(s5_in, scm[r:r + SCH, i, k, DH * g:DH * g + DH], cv[k, j, g])
                small(s5_in, sd[:, :], lay("s5_d", l).rearrange("(k p) -> p k", p=P))
                weights(1)
                for i, c in enumerate("kv"):
                    for m in range(0, CSTR, 8):
                        small(mix_in, w1[:, i, m:m + 8, :],
                              lay(f"cmp_{c}_w1", l).rearrange("(m p) n -> p m n", p=P)[:, m:m + 8, :])
                    small(mix_in, cpos[:, i, :], lay(f"cmp_{c}_pos", l).rearrange("(m e) d -> (e d) m", e=2))
                    small(mix_in, w2[:, i, :], lay(f"cmp_{c}_w2", l))
                small(mix_in, w_ng[:, :, :], lay("w_in", l)[:, C_G:C_G + 24].rearrange("(k p) n -> p k n", p=P))
                small(mix_in, q_gain[:, :], lay("q_gain", l).partition_broadcast(P))
                small(mix_in, k_gain[:, :], lay("k_gain", l).partition_broadcast(P))
                small(mix_in, w_r[:, :, 0:4], lay("router_group", l).rearrange("(k p) n -> p k n", p=P))
                small(mix_in, w_r[:, :, 4:NR], lay("router_expert", l).rearrange("(k p) n -> p k n", p=P))
                small(mix_in, b_r[:, 0:4], lay("router_group_bias", l).partition_broadcast(P))
                small(mix_in, b_r[:, 4:NR], lay("router_expert_bias", l).partition_broadcast(P))
                small(mix_in, w_glu, lay("s5_glu", l).rearrange("(k p) n -> p k n", p=P))
                for c in range(2, len(CHUNKS)):
                    weights(c)

                sp.wait_ge(norm["ffn", "h"], NT)
                sp.dma_start(h_rows.rearrange("(t p) d -> p t d", p=P), h[:, :, :]).then_inc(h_out, 16)
                def load_pair(p, it):
                    for names in (("gate", "up"), ("down",)):
                        for e, n in [(e, n) for e in range(2) for n in names]:
                            row = (l * NE + p * 2 + e)
                            dst, free, landed = {"gate": (gate_w[e], gate_free[e], gate_in[e]),
                                                 "up": (up_w[e], up_free[e], up_in[e]),
                                                 "down": (down_w[e], down_free[e], down_in[e])}[n]
                            src = a["expert_" + n][bass.ds(row, 1), :, :].rearrange("o (k p) n -> p (o k) n", p=P)
                            if it is not None:
                                wait_reg(sp, free, it)
                            sp.dma_start(dst, src).then_inc(landed, 16)

                sp.wait_ge(x_mixed, 4 * NT)
                load_pair(0, None)
                sp.wait_ge(rounds_ready, 1)
                nb = sp.value_load(rounds[0:1, 0:1], min_val=1, max_val=S // CAP)
                with sp.Fori(1, nb * PAIRS) as it:
                    wait_reg(sp, combined, it // PAIRS + 1)
                    load_pair(it % PAIRS, it)
                close_layer(sp, l)
            sp.dma_start(out[0].rearrange("(t p) d -> p t d", p=P), x[:, :, :]).then_inc(out_sem, 16)
            sp.wait_ge(out_sem, 16)

        N_S5_IN = 16 * (2 + 2 + 2 + 32 // 2 * 2 + 1)
        N_MIX_IN = 16 * (8 + 1 + 2 + 2 + 2 + 1)

        def ring_count(c):
            return sum(16 * HEADS if CHUNKS[i][0] == "proj_nsa" else 16 for i in range(c % NRING, c + 1, NRING))

        @block.tensor
        def _(pe):
            def chunk(c):
                pe.wait_ge(ring_in[c % NRING], ring_count(c))
                return ring[c % NRING].rearrange("p (k n) -> p k n", k=CHUNKS[c][2])

            def turn(which):
                for t in range(NT):
                    pe.wait_ge(norm[which, "h"], t + 1)
                    for q in range(2):
                        i = 2 * t + q
                        if i >= 4:
                            pe.wait_ge(norm[which, "hT"], i - 3)
                        for k in range(4):
                            m = pe.transpose(bank[:, i % 4, P * k:P * k + P],
                                             h[:, t, P * (4 * q + k):P * (4 * q + k) + P], ident[:, :])
                        m.then_inc(norm[which, "tr"], 1)

            def mm(dst, pairs):
                for i, (w, m) in enumerate(pairs):
                    r = pe.matmul(dst, w, m, start=(i == 0), stop=(i == len(pairs) - 1))
                return r

            def group(g):
                i = GIDX[g]
                if i >= NBANK:
                    pe.wait_ge(pj_evac, i - NBANK + 1)
                b = bank[:, i % NBANK, :]
                kind = g[0]
                if kind == "u":
                    w = chunk(0)
                    r = mm(b, [(w[:, k, P * g[1]:P * g[1] + P], hT[:, k, :]) for k in range(KD)])
                elif kind in ("kc", "vc"):
                    w = chunk(1)
                    o = P * (kind == "vc")
                    r = mm(b, [(w[:, k, o:o + P], hT[:, k, :]) for k in range(KD)])
                elif kind == "tok":
                    w = chunk(g[1])
                    r = mm(b[:, 0:CW], [(hT[:, k, P * g[2]:P * g[2] + P], w[:, k, :]) for k in range(KD)])
                elif kind == "ng":
                    for t in range(NT):
                        r = mm(b[:, 24 * t:24 * t + 24],
                               [(hT[:, k, P * t:P * t + P], w_ng[:, k, :]) for k in range(KD)])
                elif kind == "gate":
                    w = chunk(6 + g[1] // 2)
                    o = P * (g[1] % 2)
                    r = mm(b, [(w[:, k, o:o + P], hT[:, k, :]) for k in range(KD)])
                elif kind == "hid":
                    pe.wait_ge(mix_in, N_MIX_IN)
                    pe.wait_ge(pj_evac, GIDX[("vc" if g[1] else "kc", 0)] + 1)
                    for hh in range(KVH):
                        src = k2[:, 2 * g[1] + hh, :]
                        r = mm(b[:, NCMP * hh:NCMP * hh + NCMP],
                               [(w1[:, g[1], m, :], src[:, 2 * m:2 * m + CSTR * (NCMP - 1) + 1:CSTR]) for m in range(CSTR)])
                    r = mm(b[:, 2 * NCMP:2 * NCMP + 1],
                           [(w1[:, g[1], m, :], cpos[:, g[1], m:m + 1]) for m in range(CSTR)])
                elif kind == "cmp":
                    pe.wait_ge(pj_evac, GIDX[("hid", g[1])] + 1)
                    for hh in range(KVH):
                        r = mm(b[0:NCMP, DH * hh:DH * hh + DH],
                               [(gcmp[:, g[1], NCMP * hh:NCMP * hh + NCMP], w2[:, g[1], :])])
                elif kind == "tq":
                    t = g[1]
                    pe.wait_ge(qk_ready, t + 1)
                    for k in range(GRP):
                        r = pe.transpose(b[:, P * k:P * k + P], qn[:, t % 2, P * k:P * k + P], ident[:, :])
                elif kind == "tk":
                    t = g[1]
                    for k in range(2):
                        r = pe.transpose(b[:, P * k:P * k + P], qn[:, t % 2, 512 + P * k:512 + P * k + P], ident[:, :])
                elif kind == "tkc":
                    pe.wait_ge(kcn_ready, 1)
                    r = pe.transpose(b[:, 0:NCMP], kcn[0:NCMP, :], ident[0:NCMP, 0:NCMP])
                elif kind == "z":
                    pe.wait_ge(gelu_done, 2)
                    m = g[1]
                    r = mm(b, [(w_glu[:, k, P * m:P * m + P], gT[:, k, :]) for k in range(2)])
                r.then_inc(pj_done, 1)

            def s5_step(g):
                kind, t = g
                if kind == "s5t":
                    pe.wait_ge(bb_ready, 4)
                    pe.wait_ge(s5_in, N_S5_IN)
                    for i in range(2):
                        for k in range(2):
                            c = P * (2 * i + k)
                            pe.transpose(bank[:, 4, c:c + P],
                                         bbw[:, i, 4 * k:4 * k + 4, :].rearrange("p a b -> p (a b)"), ident[:, :])
                    for i in range(2):
                        for k in range(2):
                            c = P * (2 * i + k)
                            r = pe.transpose(bank[:, 5, c:c + P], scm[:, i, k, :], ident[:, :])
                    r.then_inc(s5_tr, 1)
                    return
                k, r0 = t // 4, 32 * (t % 4)
                if kind == "bu":
                    if t == 0:
                        pe.wait_ge(s5_mat, 3)
                        pe.wait_ge(pj_evac, 2)
                    else:
                        pe.wait_ge(bu_copied, t)
                    for i in range(2):
                        r = pe.matmul(bank[:, 4 + i, :], bT[r0:r0 + 32, i, k, :], uT[r0:r0 + 32, k, :],
                                      start=True, stop=True, tile_position=(r0, 0))
                    r.then_inc(bu_done, 1)
                else:
                    pe.wait_ge(scan_done, t + 1)
                    for i in range(2):
                        r = pe.matmul(bank[r0:r0 + 32, 6 + k, :], cT[:, i, k, r0:r0 + 32], s5out[:, t % 2, i, :],
                                      start=(i == 0), stop=(i == 1))
                    r.then_inc(y_done, 1)

            def scores(n):
                qt, j, br = UNITS[n]
                nk = NCMP if br == CMPB else P * (qt + 1)
                keys = kcT[:, 0:NCMP] if br == CMPB else kT[:, br - 1, 0:nk]
                for g in range(GRP):
                    if n:
                        pe.wait_ge(exp_done, GRP * (n - 1) + g + 1)
                    rows = slice(DH * j, DH * j + DH)
                    pe.matmul(bank[:, g, 0:nk], qT[rows, g, P * qt:P * qt + P], keys[rows, :], start=True, stop=False)
                    if br == CMPB:
                        r = pe.matmul(bank[:, g, 0:nk], ident[:, :], cmpmask[:, qt, 0:NCMP], start=False, stop=True)
                    else:
                        r = pe.matmul(bank[:, g, P * qt:nk], ident[:, :], causal[:, :], start=False, stop=True)
                    r.then_inc(score_done, 1)

            def values(n):
                qt, j, br = UNITS[n]
                c0 = first_tr(n)
                nt = key_tiles(UNITS[n])
                w = NCMP if br == CMPB else P
                u = n // 3

                def turn_tile(kt):
                    c = c0 + kt
                    if c >= 2:
                        pe.wait_ge(evac_act if c % 2 == 0 else evac_dve, c // 2)
                    for g in range(GRP):
                        if kt == 0:
                            pe.wait_ge(p_ready, GRP * n + g + 1)
                        r = pe.transpose(bank[0:w, 4 + c % 2, P * g:P * g + P],
                                         prob[:, n % 2, g, P * kt:P * kt + w], ident[:, :])
                    r.then_inc(tr_done, 1)

                def add_tile(kt):
                    c = c0 + kt
                    pe.wait_ge(evac_act if c % 2 == 0 else evac_dve, c // 2 + 1)
                    v = (vcs[0:NCMP, DH * j:DH * j + DH] if br == CMPB else
                         raw[:, kt, 640 + 256 * (br - 1) + DH * j:640 + 256 * (br - 1) + DH * j + DH])
                    r = pe.matmul(bank[DH * j:DH * j + DH, 6 + u % 2, :], v, pT[0:w, c % 4, :],
                                  start=(br == CMPB), stop=(br == WIN and kt == nt - 1))
                    r.then_inc(pv_done, 1)

                if br == CMPB and u >= 2:
                    pe.wait_ge(o_evac, u - 1)
                turn_tile(0)
                for kt in range(nt):
                    if kt + 1 < nt:
                        turn_tile(kt + 1)
                    add_tile(kt)

            def merge():
                ws = chunk(14)
                for m in range(KD):
                    wa = chunk(15 + m // 4)
                    o = P * (m % 4)
                    if m >= 2:
                        pe.wait_ge(merged, m - 1)
                    mm(bank[:, 2 * (m % 2), :], [(wa[:, k, o:o + P], oT[:, k, :]) for k in range(4)])
                    r = mm(bank[:, 2 * (m % 2) + 1, :], [(ws[:, k, P * m:P * m + P], sT[:, k, :]) for k in range(2)])
                    r.then_inc(merge_mm, 1)

            def project_out():
                pe.wait_ge(merged, KD)
                for j in range(4):
                    w = chunk(17 + j)
                    for t in range(NT):
                        i = NT * j + t
                        if i >= 4:
                            pe.wait_ge(x_mixed, i - 3)
                        r = mm(bank[:, 4 + i % 4, 0:CW],
                               [(mergedT[:, k, P * t:P * t + P], w[:, k, :]) for k in range(KD)])
                        r.then_inc(out_mm, 1)

            def route():
                pe.wait_ge(norm["ffn", "hT"], 8)
                pe.wait_ge(mix_in, N_MIX_IN)
                for t in range(NT):
                    r = mm(bank[:, 4, NR * t:NR * t + NR],
                           [(hT[:, k, P * t:P * t + P], w_r[:, k, :]) for k in range(KD)])
                r.then_inc(logit_mm, 1)
                pe.wait_ge(r_member, 1)
                for t in range(NT):
                    mm(bank[:, 5, NE * t:NE * t + NE],
                       [(ones[:, :], member[:, i, :]) for i in range(t)] + [(before[:, :], member[:, t, :])])
                r = mm(bank[:, 5, NE * NT:NE * NT + NE], [(ones[:, :], member[:, i, :]) for i in range(NT)])
                r.then_inc(prefix_mm, 1)

            def experts():
                pe.wait_ge(rounds_ready, 1)
                nb = pe.value_load(rounds[0:1, 0:1], min_val=1, max_val=S // CAP)
                with pe.Fori(0, nb) as b:
                    with pe.Fori(0, PAIRS) as p:
                        it = b * PAIRS + p
                        wait_reg(pe, rows_in, it * 16 + 16)
                        for k in range(KD):
                            r = pe.transpose(bank[:, k // 4, P * (k % 4):P * (k % 4) + P],
                                             xrow[:, P * k:P * k + P], ident[:, :])
                            if k % 4 == 3:
                                r.then_inc(xt_done, 1)
                        wait_reg(pe, xg_ready, it * 2 + 3)

                        def into(e, w, landed, free, o):
                            wait_reg(pe, landed, it * 16 + 16)
                            mm(bank[CAP * e:CAP * e + CAP, 2 + o, :],
                               [(xg[:, k, CAP * e:CAP * e + CAP], w[:, k, :]) for k in range(KD)]).then_inc(free, 1)

                        def turn_act(e):
                            wait_reg(pe, act_ready, it * 2 + (e + 1))
                            rows = slice(CAP * e, CAP * e + CAP)
                            for f in range(KF):
                                r = pe.transpose(bank[:, 6 + e, CAP * f:CAP * f + CAP], hid[rows, P * f:P * f + P],
                                                 ident[rows, rows])
                            r.then_inc(at_done, 1)

                        def down(e):
                            wait_reg(pe, at_ready, it * 2 + (e + 1))
                            wait_reg(pe, down_in[e], it * 16 + 16)
                            for half in range(2):
                                r = mm(bank[CAP * e:CAP * e + CAP, 4 + half, :],
                                       [(actT[e][:, f, :], down_w[e][:, f, 512 * half:512 * half + 512])
                                        for f in range(KF)])
                            r.then_inc(down_free[e], 1)

                        into(0, gate_w[0], gate_in[0], gate_free[0], 0)
                        into(0, up_w[0], up_in[0], up_free[0], 1)
                        into(1, gate_w[1], gate_in[1], gate_free[1], 0)
                        turn_act(0)
                        into(1, up_w[1], up_in[1], up_free[1], 1)
                        wait_reg(pe, y_ready, it + 1)
                        down(0)
                        turn_act(1)
                        down(1)

            pe.wait_ge(pool_const, N_POOL)
            pe.wait_ge(dve_const, N_DVE_CONST)
            with pe.Fori(0, DEPTH) as l:
                turn("mix")
                pe.wait_ge(norm["mix", "hT"], 8)
                for g in SEQ:
                    if g[0] in ("s5t", "bu", "y"):
                        s5_step(g)
                    else:
                        group(g)
                pe.wait_ge(pj_evac, len(GROUPS))
                scores(0)
                for n in range(len(UNITS)):
                    if n + 1 < len(UNITS):
                        scores(n + 1)
                    values(n)
                pe.wait_ge(o_evac, 8)
                pe.wait_ge(sT_ready, 2)
                merge()
                project_out()
                turn("ffn")
                route()
                experts()
                close_layer(pe, l)

        @block.scalar
        def _(act):
            def sums(which):
                for t in range(NT):
                    if which == "ffn":
                        act.wait_ge(x_mixed, 3 * NT + t + 1)
                    if t:
                        act.wait_ge(norm[which, "sums"], t)
                    act.activation(junk, x[:, t, :], ACT.Square, accum_out=stat[:, 0, t:t + 1])\
                       .then_inc(norm[which, "sums"], 1)
                act.wait_ge(norm[which, "mean"], 1)
                act.activation(stat[:, 2, :], stat[:, 1, :], ACT.Sqrt).then_inc(norm[which, "root"], 1)

            def evac(g):
                i = GIDX[g]
                act.wait_ge(pj_done, i + 1)
                b = bank[:, i % NBANK, :]
                kind = g[0]
                if kind == "u":
                    r = act.activation(uT[:, g[1], :], b, ACT.Copy)
                elif kind in ("kc", "vc"):
                    o = 2 * (kind == "vc")
                    for hh in range(KVH):
                        rows = slice(DH * hh, DH * hh + DH)
                        act.activation(k2[0:DH, o + hh, :], b[rows, :], ACT.Copy)
                        r = act.activation(k2[DH:P, o + hh, 0:S - 1], b[rows, 1:S], ACT.Copy)
                elif kind == "tok":
                    r = act.activation(raw[:, g[2], CW * (g[1] - 2):CW * (g[1] - 1)], b[:, 0:CW], ACT.Copy)
                elif kind == "ng":
                    r = act.activation(gsig.rearrange("p t n -> p (t n)"), b[:, 0:24 * NT], ACT.Sigmoid)
                elif kind == "gate":
                    r = act.activation(gates[:, g[1], :], b, ACT.Sigmoid)
                elif kind == "hid":
                    act.activation(hb[:, g[1]:g[1] + 1], b[:, 2 * NCMP:2 * NCMP + 1], ACT.Copy).then_inc(act_chain, 1)
                    act.wait_ge(act_chain, g[1] + 1)
                    r = act.activation(gcmp[:, g[1], 0:2 * NCMP], b[:, 0:2 * NCMP], ACT.Gelu_apprx_tanh,
                                       bias=hb[:, g[1]:g[1] + 1])
                elif kind == "cmp":
                    r = act.activation((kcraw if g[1] == 0 else vcs)[0:NCMP, :], b[0:NCMP, 0:P], ACT.Copy)
                elif kind == "tq":
                    r = act.activation(qT[:, :, P * g[1]:P * g[1] + P], b.rearrange("p (g t) -> p g t", g=GRP), ACT.Copy)
                elif kind == "tk":
                    r = act.activation(kT[:, :, P * g[1]:P * g[1] + P],
                                       b[:, 0:2 * P].rearrange("p (g t) -> p g t", g=2), ACT.Copy)
                elif kind == "tkc":
                    r = act.activation(kcT[:, 0:NCMP], b[:, 0:NCMP], ACT.Copy)
                elif kind == "z":
                    if g[1] < 2:
                        r = act.activation(zval[:, g[1], :], b, ACT.Copy)
                    else:
                        r = act.activation(zsig[:, g[1] - 2, :], b, ACT.Sigmoid)
                r.then_inc(pj_evac, 1)

            def exps(n):
                qt, j, br = UNITS[n]
                nk = NCMP if br == CMPB else P * (qt + 1)
                if n == 0:
                    act.wait_ge(sT_ready, 2)
                if n >= 2:
                    act.wait_ge(tr_done, first_tr(n - 1))
                for g in range(GRP):
                    act.wait_ge(max_ready, GRP * n + g + 1)
                    act.activation(prob[:, n % 2, g, 0:nk], bank[:, g, 0:nk], ACT.Exp, scale=SCALE,
                                   bias=nbias[:, n % 2, g:g + 1], accum_out=rsum[:, n % 2, g:g + 1])\
                       .then_inc(exp_done, 1)

            def evac_probs(n):
                qt, j, br = UNITS[n]
                w = NCMP if br == CMPB else P
                for kt in range(key_tiles(UNITS[n])):
                    c = first_tr(n) + kt
                    if c % 2:
                        continue
                    act.wait_ge(tr_done, c + 1)
                    if c >= 4:
                        act.wait_ge(pv_done, c - 3)
                    act.activation(pT[0:w, c % 4, :], bank[0:w, 4, :], ACT.Copy).then_inc(evac_act, 1)
                if br == WIN:
                    act.wait_ge(pv_done, first_tr(n + 1))
                    rows = slice(DH * j, DH * j + DH)
                    act.activation(oT[rows, :, P * qt:P * qt + P],
                                   bank[rows, 6 + (n // 3) % 2, :].rearrange("p (g t) -> p g t", g=GRP), ACT.Copy)\
                       .then_inc(o_evac, 1)

            act.wait_ge(rope_angle, 2)
            act.activation(sint[:, :, :], ang[:, :, :], ACT.Sin).then_inc(rope_done, 1)
            act.activation(cost[:, :, :], angc[:, :, :], ACT.Sin).then_inc(rope_done, 1)
            act.wait_ge(x_in, 48)
            with act.Fori(0, DEPTH) as l:
                sums("mix")
                act.wait_ge(s5_in, N_S5_IN)
                act.activation(s5v[:, 0, :], sa[:, 2, :], ACT.Exp).then_inc(s5_dt, 1)
                act.wait_ge(s5_ang, 1)
                act.activation(s5v[:, 4, :], s5v[:, 1, :], ACT.Exp).then_inc(s5_trig, 1)
                act.wait_ge(s5_ang, 3)
                act.activation(s5v[:, 5, :], s5v[:, 2, :], ACT.Sin).then_inc(s5_trig, 1)
                act.activation(s5v[:, 6, :], s5v[:, 3, :], ACT.Sin).then_inc(s5_trig, 1)
                act.wait_ge(norm["mix", "tr"], 8)
                for g in GROUPS:
                    if g == ("z", 0):
                        for k in range(2):
                            act.wait_ge(ypre_ready, k + 1)
                            act.activation(gT[:, k, :], gT[:, k, :], ACT.Gelu_apprx_tanh).then_inc(gelu_done, 1)
                    evac(g)
                    if g == ("gate", 3):
                        act.wait_ge(qk_mean, 1)
                        act.activation(qstat[:, 2, :], qstat[:, 1, :], ACT.Sqrt).then_inc(qk_root, 1)
                exps(0)
                for n in range(len(UNITS)):
                    if n + 1 < len(UNITS):
                        exps(n + 1)
                    evac_probs(n)
                sums("ffn")
                for i in range(2):
                    act.wait_ge(r_exp_in, i + 1)
                    if i == 0:
                        act.activation(rt[:, 7, :, 0:4], rt[:, 6, :, 0:4], ACT.Exp).then_inc(r_exp, 1)
                    else:
                        act.activation(rs[:, 7, :], rs[:, 6, :], ACT.Exp).then_inc(r_exp, 1)
                act.wait_ge(rounds_ready, 1)
                nb = act.value_load(rounds[0:1, 0:1], min_val=1, max_val=S // CAP)
                act.sem_inc(y_ready, 1)
                act.sem_inc(y_out, 16)
                with act.Fori(0, nb) as b:
                    wait_reg(act, combined, b + 1)
                    with act.Fori(0, PAIRS) as p:
                        it = b * PAIRS + p
                        for e in range(2):
                            wait_reg(act, up_free[e], it + 1)
                            rows = slice(CAP * e, CAP * e + CAP)
                            act.activation(silu[rows, :], bank[rows, 2, :], ACT.Silu).then_inc(silu_done, 1)
                            wait_reg(act, at_done, it * 2 + (e + 1))
                            act.activation(actT[e].rearrange("p a b -> p (a b)"), bank[:, 6 + e, 0:KF * CAP],
                                           ACT.Copy).then_inc(at_ready, 1)
                        wait_reg(act, down_free[1], it + 1)
                        wait_reg(act, y_out, it * 16 + 16)
                        act.activation(yslot[:, 0:512], bank[:, 4, :], ACT.Copy)
                        act.activation(yslot[:, 512:1024], bank[:, 5, :], ACT.Copy).then_inc(y_ready, 1)
                        dst = y_rows.rearrange("(i p) d -> i p d", p=P)[bass.ds(p, 1), :, :].rearrange("o p d -> (o p) d")
                        wait_reg(act, y_ready, it + 2)
                        act.dma_start(dst, yslot).then_inc(y_out, 16)
                close_layer(act, l)

        @block.vector
        def _(dve):
            TT, TS, STT = dve.tensor_tensor, dve.tensor_scalar, dve.scalar_tensor_tensor

            def bc(ap, n):
                shape = list(ap.shape)
                return ap.unsqueeze(len(shape)).broadcast_to(shape + [n])

            def mid(ap, n):
                p, m = ap.shape
                return ap.unsqueeze(1).broadcast_to([p, n, m])

            def reduce_angle(link, src, k, sin_in, cos_in, last):
                link.do(TS(k, src, 1.0 / TWO_PI, ROUND, ALU.mult, ALU.add))
                link.do(TS(k, k, ROUND, None, ALU.subtract))
                link.do(STT(sin_in, k, -PI_1, src, ALU.mult, ALU.add))
                link.do(STT(sin_in, k, -PI_2, sin_in, ALU.mult, ALU.add))
                link.do(STT(sin_in, k, -PI_3, sin_in, ALU.mult, ALU.add))
                link.do(TS(cos_in, sin_in, np.pi / 2, None, ALU.add))
                link.do(TS(k, cos_in, float(np.pi), TWO_PI, ALU.is_gt, ALU.mult))
                link.do(TT(cos_in, cos_in, k, ALU.subtract))
                TS(cos_in, cos_in, PI_MAX, -PI_MAX, ALU.min, ALU.max).then_inc(last, 1)
                TS(sin_in, sin_in, PI_MAX, -PI_MAX, ALU.min, ALU.max).then_inc(last, 1)

            for tile in (scm[:, :, :, :], bbw[:, :, :, :], scanbuf):
                dve.memset(tile, 0.0).then_inc(dve_const, 1)
            dve.memset(pos_i[:, :], 0).then_inc(dve_const, 1)
            inv = (np.float32(500000.0) ** (-np.arange(0, 16, 2, dtype=np.float32) / np.float32(16)))
            for i in range(HALF):
                m = dve.memset(invf[:, i:i + 1], float(inv[i]))
            m.then_inc(dve_const, 1)
            for i in range(NE):
                m = dve.memset(desc[:, i:i + 1], float(NE - i))
            m.then_inc(dve_const, 1)
            for i in range(8):
                m = dve.memset(thr[:, i:i + 1], float(CAP * (i + 1)))
            m.then_inc(dve_const, 1)
            dve.memset(k2, 0.0).then_inc(dve_const, 1)
            for i in range(NE):
                m = dve.memset(eid[:, i:i + 1], float(i))
            m.then_inc(dve_const, 1)
            dve.wait_ge(pool_const, N_POOL)
            dve.wait_ge(dve_const, N_DVE_CONST)
            dve.wait_ge(x_in, 48)
            link0 = Chain(dve, sem("rope_chain", False))
            link0.do(dve.tensor_copy(posf[:, :], pos_i[:, :]))
            link0.do(TT(ang[:, :, :], bc(posf[:, :], HALF), mid(invf[:, :], 5), ALU.mult))
            link0.do(dve.tensor_copy(cost[:, :, :], ang[:, :, :]))
            reduce_angle(link0, cost[:, :, :], angk[:, :, :], ang[:, :, :], angc[:, :, :], rope_angle)
            dve.wait_ge(rope_done, 2)

            with dve.Fori(0, DEPTH) as l:
                link = Chain(dve, dve_chain)
                do = link.do

                def normalise(which, gain):
                    dve.wait_ge(norm[which, "sums"], NT)
                    TS(stat[:, 1, :], stat[:, 0, :], 1.0 / D, EPS, ALU.mult, ALU.add).then_inc(norm[which, "mean"], 1)
                    dve.wait_ge(norm[which, "root"], 1)
                    do(dve.reciprocal(stat[:, 0, :], stat[:, 2, :]))
                    for t in range(NT):
                        TS(h[:, t, :], x[:, t, :], stat[:, 0, t:t + 1], None, ALU.mult).then_inc(norm[which, "h"], 1)
                    dve.wait_ge(gain_in, 32)
                    for i in range(2 * NT):
                        t, q = i // 2, i % 2
                        dve.wait_ge(norm[which, "tr"], i + 1)
                        TT(hT[:, 4 * q:4 * q + 4, P * t:P * t + P], bank[:, i % 4, :].rearrange("p (k t) -> p k t", k=4),
                           bc(gain[:, 4 * q:4 * q + 4], P), ALU.mult).then_inc(norm[which, "hT"], 1)

                normalise("mix", g_mix)

                v = lambda i: s5v[:, i, :]
                DT, LD, SIN, COSI, MAG, SN, CS, LRE, T0, T1, T2, DEN, FRE, FIM, ANG, KK = range(16)
                dve.wait_ge(s5_in, N_S5_IN)
                do(TS(v(LRE), sa[:, 0, :], -1e-4, None, ALU.min))
                dve.wait_ge(s5_dt, 1)
                TT(v(LD), v(LRE), v(DT), ALU.mult).then_inc(s5_ang, 1)
                do(TT(v(ANG), sa[:, 1, :], v(DT), ALU.mult))
                reduce_angle(link, v(ANG), v(KK), v(SIN), v(COSI), s5_ang)
                dve.wait_ge(s5_trig, 3)
                pre, pim, nim = (lambda k: pw[:, k, 0, :]), (lambda k: pw[:, k, 1, :]), (lambda k: pw[:, k, 2, :])
                do(TT(pre(0), v(MAG), v(CS), ALU.mult))
                do(TT(pim(0), v(MAG), v(SN), ALU.mult))
                do(TT(v(T0), v(LRE), v(LRE), ALU.mult))
                do(TT(v(T1), sa[:, 1, :], sa[:, 1, :], ALU.mult))
                do(TT(v(DEN), v(T0), v(T1), ALU.add))
                do(dve.reciprocal(v(DEN), v(DEN)))
                do(TS(v(T2), pre(0), 1.0, None, ALU.subtract))
                do(TT(v(T0), v(T2), v(LRE), ALU.mult))
                do(TT(v(T1), pim(0), sa[:, 1, :], ALU.mult))
                do(TT(v(T0), v(T0), v(T1), ALU.add))
                do(TT(v(FRE), v(T0), v(DEN), ALU.mult))
                do(TT(v(T0), pim(0), v(LRE), ALU.mult))
                do(TT(v(T1), v(T2), sa[:, 1, :], ALU.mult))
                do(TT(v(T0), v(T0), v(T1), ALU.subtract))
                do(TT(v(FIM), v(T0), v(DEN), ALU.mult))
                for i, (f, m) in enumerate(((FRE, 0), (FIM, 1), (FRE, 1), (FIM, 0))):
                    do(TT(bbt[:, i, :, :], bc(v(f), SCH), sbm[:, m, :, :], ALU.mult))
                for i, op in ((0, ALU.subtract), (1, ALU.add)):
                    for g in range(2):
                        rows = slice(DH * g, DH * g + DH)
                        TT(bbw[rows, i, :, SCH * g:SCH * g + SCH], bbt[rows, 2 * i, :, :], bbt[rows, 2 * i + 1, :, :],
                           op).then_inc(bb_ready, 1)
                dve.wait_ge(s5_tr, 1)
                dve.tensor_copy(bT[:, :, :, :].rearrange("p a b c -> p (a b c)"), bank[:, 4, :]).then_inc(s5_mat, 1)
                dve.tensor_copy(cT[:, 0, :, :].rearrange("p b c -> p (b c)"), bank[:, 5, 0:2 * P]).then_inc(s5_mat, 1)
                TS(cT[:, 1, :, :].rearrange("p b c -> p (b c)"), bank[:, 5, 2 * P:4 * P], -1.0, None, ALU.mult)\
                    .then_inc(s5_mat, 1)

                for k in range(9):
                    do(TS(nim(k), pim(k), -1.0, None, ALU.mult))
                    if k < 8:
                        do(TT(v(T0), pre(k), pre(k), ALU.mult))
                        do(TT(v(T1), pim(k), pim(k), ALU.mult))
                        do(TT(pre(k + 1), v(T0), v(T1), ALU.subtract))
                        do(TT(v(T2), pre(k), pim(k), ALU.mult))
                        do(TS(pim(k + 1), v(T2), 2.0, None, ALU.mult))

                def scan(T):
                    A = [scanbuf[:, 0, :], scanbuf[:, 1, :]]
                    B = [scanbuf[:, 2, :], scanbuf[:, 3, :]]
                    if T:
                        dve.wait_ge(scan_done, T)
                    dve.wait_ge(bu_done, T + 1)
                    for i in range(2):
                        r = dve.tensor_copy(A[i][:, PAD:PAD + S], bank[:, 4 + i, :])
                        if i == 0:
                            last = [link(r), 0]
                        else:
                            r.then_inc(bu_copied, 1)
                    for k in range(9):
                        sh = 1 << k
                        src = A if k % 2 == 0 else B
                        ar, ai, ni = (pw[:, k, i, T:T + 1] for i in range(3))
                        cur = [s[:, PAD:PAD + S] for s in src]
                        old = [s[:, PAD - sh:PAD + S - sh] for s in src]
                        if k == 8:
                            dst = [s5out[:, T % 2, i, :] for i in range(2)]
                            if T >= 2:
                                dve.wait_ge(y_done, T - 1)
                        else:
                            dst = [s[:, PAD:PAD + S] for s in (B if k % 2 == 0 else A)]
                        if k == 0:
                            dve.wait_ge(bu_copied, T + 1)
                        else:
                            link.sync(last[1])
                        n0 = link(STT(dst[0], old[0], ar, cur[0], ALU.mult, ALU.add))
                        n1 = link(STT(dst[1], old[1], ar, cur[1], ALU.mult, ALU.add))
                        link.sync(n0)
                        r = STT(dst[0], old[1], ni, dst[0], ALU.mult, ALU.add)
                        last[0] = link(r)
                        link.sync(n1)
                        r = STT(dst[1], old[0], ai, dst[1], ALU.mult, ALU.add)
                        if k == 8:
                            r.then_inc(scan_done, 1)
                        else:
                            last[1] = link(r)

                def sums_qk():
                    dve.wait_ge(pj_evac, GIDX[("ng", 0)] + 1)
                    for t in range(NT):
                        do(TT(sq[:, :], raw[:, t, :], raw[:, t, :], ALU.mult))
                        do(dve.tensor_reduce(qstat[:, 0, 16 * t:16 * t + 16],
                                             sq[:, :].rearrange("p (n d) -> p n d", d=DH), AX.X, ALU.add))
                    do(TT(sq[0:NCMP, 0:P], kcraw[0:NCMP, :], kcraw[0:NCMP, :], ALU.mult))
                    do(dve.tensor_reduce(qstat[0:NCMP, 0, 64:66],
                                         sq[0:NCMP, 0:P].rearrange("p (n d) -> p n d", d=DH), AX.X, ALU.add))
                    TS(qstat[:, 1, :], qstat[:, 0, :], 1.0 / DH, EPS, ALU.mult, ALU.add).then_inc(qk_mean, 1)

                def rope(X, n, rows, col):
                    x1, x2 = X[:, :, 0:HALF], X[:, :, HALF:2 * HALF]
                    c, s = mid(cost[rows, col, :], n), mid(sint[rows, col, :], n)
                    for i, (u, w) in enumerate(((x1, c), (x2, s), (x2, c), (x1, s))):
                        link(TT(rtmp[rows, i, 0:n, :], u, w, ALU.mult))
                    link.sync()
                    r1 = TT(x1, rtmp[rows, 0, 0:n, :], rtmp[rows, 1, 0:n, :], ALU.subtract)
                    r2 = TT(x2, rtmp[rows, 2, 0:n, :], rtmp[rows, 3, 0:n, :], ALU.add)
                    return r1, r2

                def norm_qk(t):
                    if t >= 2:
                        dve.wait_ge(pj_done, GIDX[("tk", t - 2)] + 1)
                    r = qstat[:, 0, 16 * t:16 * t + 16]
                    Q = qn[:, t % 2, 0:512]
                    K = qn[:, t % 2, 512:768]
                    for hh in range(2):
                        link(TT(Q.rearrange("p (g h d) -> p h g d", g=GRP, h=2)[:, hh], 
                                raw[:, t, 256 * hh:256 * hh + 256].rearrange("p (g d) -> p g d", d=DH),
                                bc(r[:, 4 * hh:4 * hh + 4], DH), ALU.mult))
                        link(TT(K[:, P * hh:P * hh + P].rearrange("p (g d) -> p g d", d=DH),
                                raw[:, t, 512 + 256 * hh:640 + 256 * hh].rearrange("p (g d) -> p g d", d=DH),
                                bc(r[:, 8 + 4 * hh:10 + 4 * hh], DH), ALU.mult))
                    link.sync()
                    Q3 = Q.rearrange("p (g d) -> p g d", d=DH)
                    K3 = K.rearrange("p (g d) -> p g d", d=DH)
                    link(TT(Q3, Q3, mid(q_gain[:, :], 8), ALU.mult))
                    do(TT(K3, K3, mid(k_gain[:, :], 4), ALU.mult))
                    r1, r2 = rope(qn[:, t % 2, :].rearrange("p (g d) -> p g d", d=DH), 12, slice(0, P), t)
                    link(r1)
                    r2.then_inc(qk_ready, 1)

                for T in range(6):
                    scan(T)
                sums_qk()
                for T in range(6, NST):
                    scan(T)
                for k in range(2):
                    dve.wait_ge(y_done, 4 * k + 4)
                    STT(gT[:, k, :], uT[:, k, :], sd[:, k:k + 1], bank[:, 6 + k, :], ALU.mult, ALU.add)\
                        .then_inc(ypre_ready, 1)
                dve.wait_ge(qk_root, 1)
                do(dve.reciprocal(qstat[:, 0, :], qstat[:, 2, :]))
                dve.wait_ge(mix_in, N_MIX_IN)
                for t in range(NT):
                    norm_qk(t)
                K3 = kcn[0:NCMP, :].rearrange("p (g d) -> p g d", d=DH)
                do(TT(K3, kcraw[0:NCMP, :].rearrange("p (g d) -> p g d", d=DH), bc(qstat[0:NCMP, 0, 64:66], DH), ALU.mult))
                do(TT(K3, K3, mid(k_gain[0:NCMP, :], 2), ALU.mult))
                r1, r2 = rope(K3, 2, slice(0, NCMP), NT)
                link(r1)
                r2.then_inc(kcn_ready, 1)
                dve.wait_ge(pj_evac, GIDX[("z", 3)] + 1)
                for m in range(2):
                    TT(sT[:, m, :], zval[:, m, :], zsig[:, m, :], ALU.mult).then_inc(sT_ready, 1)

                def maxima(n):
                    qt, j, br = UNITS[n]
                    nk = NCMP if br == CMPB else P * (qt + 1)
                    for g in range(GRP):
                        dve.wait_ge(score_done, GRP * n + g + 1)
                        do(dve.tensor_reduce(nmax[:, n % 2, g:g + 1], bank[:, g, 0:nk], AX.X, ALU.max))
                        TS(nbias[:, n % 2, g:g + 1], nmax[:, n % 2, g:g + 1], -SCALE, None, ALU.mult)\
                            .then_inc(max_ready, 1)

                def weigh(n):
                    qt, j, br = UNITS[n]
                    nk = NCMP if br == CMPB else P * (qt + 1)
                    s = rscale[:, n % 2, :]
                    dve.wait_ge(exp_done, GRP * n + GRP)
                    do(dve.reciprocal(s, rsum[:, n % 2, :]))
                    gv = gsig[:, qt, 3 * GRP * j + br:3 * GRP * j + br + 3 * (GRP - 1) + 1:3]
                    do(TT(s, s, gv, ALU.mult))
                    if br == CMPB and qt == 0:
                        do(TS(s, s, some[:, 0:1], None, ALU.mult))
                    for g in range(GRP):
                        pr = prob[:, n % 2, g, 0:nk]
                        TS(pr, pr, s[:, g:g + 1], None, ALU.mult).then_inc(p_ready, 1)

                def evac_probs(n):
                    w = NCMP if UNITS[n][2] == CMPB else P
                    for kt in range(key_tiles(UNITS[n])):
                        c = first_tr(n) + kt
                        if c % 2 == 0:
                            continue
                        dve.wait_ge(tr_done, c + 1)
                        if c >= 4:
                            dve.wait_ge(pv_done, c - 3)
                        dve.tensor_copy(pT[0:w, c % 4, :], bank[0:w, 5, :]).then_inc(evac_dve, 1)

                maxima(0)
                for n in range(len(UNITS)):
                    weigh(n)
                    if n + 1 < len(UNITS):
                        maxima(n + 1)
                    evac_probs(n)

                for m in range(KD):
                    dve.wait_ge(merge_mm, m + 1)
                    o = 2 * (m % 2)
                    link(TT(gates[:, m, :], gates[:, m, :], bank[:, o, :], ALU.mult))
                    do(TT(gates[:, 8 + m, :], gates[:, 8 + m, :], bank[:, o + 1, :], ALU.mult))
                    TT(mergedT[:, m, :], gates[:, m, :], gates[:, 8 + m, :], ALU.add).then_inc(merged, 1)
                for i in range(4 * NT):
                    j, t = i // NT, i % NT
                    dve.wait_ge(out_mm, i + 1)
                    xv = x[:, t, CW * j:CW * j + CW]
                    TT(xv, xv, bank[:, 4 + i % 4, 0:CW], ALU.add).then_inc(x_mixed, 1)

                normalise("ffn", g_ffn)
                dve.wait_ge(logit_mm, 1)
                dve.wait_ge(mix_in, N_MIX_IN)
                do(TT(lg[:, :, :], bank[:, 4, 0:NT * NR].rearrange("p (t n) -> p t n", n=NR),
                      mid(b_r[:, :], NT), ALU.add))
                R = lambda i, n=NE: rt[:, i, :, 0:n]
                V = lambda i: rs[:, i, :]

                def first_max(src, n, hot, top):
                    do(dve.tensor_reduce(top, src, AX.X, ALU.max))
                    do(TT(hot, src, bc(top, n), ALU.is_equal))
                    do(TT(hot, hot, mid(desc[:, 0:n], NT), ALU.mult))
                    do(dve.tensor_reduce(V(11), hot, AX.X, ALU.max))
                    do(TT(hot, mid(desc[:, 0:n], NT), bc(V(11), n), ALU.is_equal))

                gl = lg[:, :, 0:4]
                first_max(gl, 4, R(0, 4), V(0))
                TT(R(6, 4), gl, bc(V(0), 4), ALU.subtract).then_inc(r_exp_in, 1)
                dve.wait_ge(r_exp, 1)
                do(dve.tensor_reduce(V(1), R(7, 4), AX.X, ALU.add))
                do(dve.reciprocal(V(1), V(1)))
                g4 = lambda ap: ap.rearrange("p t (g e) -> p t g e", g=4)
                do(TS(R(1, 4), R(0, 4), BIG, -BIG, ALU.mult, ALU.add))
                for t in range(NT):
                    link(TT(g4(R(2))[:, t], g4(lg[:, :, 4:NR])[:, t], bc(rt[:, 0, t, 0:4], 8), ALU.mult))
                link.sync()
                for t in range(NT):
                    link(TT(g4(R(2))[:, t], g4(R(2))[:, t], bc(rt[:, 1, t, 0:4], 8), ALU.add))
                link.sync()
                first_max(R(2), NE, R(3), V(2))
                do(TS(R(4), R(3), -3 * BIG, None, ALU.mult))
                do(TT(R(2), R(2), R(4), ALU.add))
                first_max(R(2), NE, R(4), V(3))
                TT(member[:, :, :], R(3), R(4), ALU.add).then_inc(r_member, 1)
                TT(V(6), V(3), V(2), ALU.subtract).then_inc(r_exp_in, 1)
                EX, RANK, ROUND_, PAIR, HALF_, IN_TAB, A_, B_ = range(8)
                pl = lambda i: place[:, i, :, :]
                for k in range(2):
                    do(TT(R(5), R(3 + k), mid(eid[:, :], NT), ALU.mult))
                    do(dve.tensor_reduce(place[:, EX, :, k], R(5), AX.X, ALU.add))
                dve.wait_ge(prefix_mm, 1)
                for k in range(2):
                    do(TT(R(5), R(3 + k), bank[:, 5, 0:NT * NE].rearrange("p (t n) -> p t n", n=NE), ALU.mult))
                    do(dve.tensor_reduce(place[:, RANK, :, k], R(5), AX.X, ALU.add))
                do(TS(pl(A_), pl(RANK), -(CAP - 1) / 2, 1.0 / CAP, ALU.add, ALU.mult))
                do(TS(pl(A_), pl(A_), ROUND, None, ALU.add))
                do(TS(pl(ROUND_), pl(A_), ROUND, None, ALU.subtract))
                do(TS(pl(A_), pl(EX), -0.5, 0.5, ALU.add, ALU.mult))
                do(TS(pl(A_), pl(A_), ROUND, None, ALU.add))
                do(TS(pl(PAIR), pl(A_), ROUND, None, ALU.subtract))
                do(STT(pl(HALF_), pl(PAIR), -2.0, pl(EX), ALU.mult, ALU.add))
                do(STT(pl(B_), pl(ROUND_), -float(CAP), pl(RANK), ALU.mult, ALU.add))
                do(STT(pl(B_), pl(HALF_), float(CAP), pl(B_), ALU.mult, ALU.add))
                do(STT(pl(A_), pl(ROUND_), float(PAIRS), pl(PAIR), ALU.mult, ALU.add))
                do(STT(pl(IN_TAB), pl(B_), float(P), pl(A_), ALU.mult, ALU.add))
                dve.tensor_copy(row_tab[:, :, :], pl(IN_TAB)).then_inc(place_ready, 1)
                do(STT(pl(HALF_), pl(PAIR), float(P), pl(B_), ALU.mult, ALU.add))
                dve.tensor_copy(row_y[:, :, :], pl(HALF_)).then_inc(place_ready, 1)
                dve.wait_ge(r_exp, 2)
                do(TS(V(4), V(7), 1.0, None, ALU.add))
                do(dve.reciprocal(V(4), V(4)))
                do(TT(V(4), V(4), V(1), ALU.mult))
                do(TT(V(5), V(4), V(7), ALU.mult))
                do(dve.tensor_reduce(cnt[:, 8:9], bank[:, 5, NT * NE:NT * NE + NE], AX.X, ALU.max))
                do(TS(cnt[:, 0:8], thr[:, :], cnt[:, 8:9], None, ALU.is_lt))
                do(dve.tensor_reduce(cnt[:, 9:10], cnt[:, 0:8], AX.X, ALU.add))
                do(TS(cnt[:, 9:10], cnt[:, 9:10], 1.0, None, ALU.add))
                dve.sem_inc(xg_ready, 1)
                dve.sem_inc(combined, 1)
                dve.tensor_copy(rounds[:, :], cnt[:, 9:10]).then_inc(rounds_ready, 1)
                dve.wait_ge(rounds_ready, 1)
                nb = dve.value_load(rounds[0:1, 0:1], min_val=1, max_val=S // CAP)

                with dve.Fori(0, nb) as b:
                    with dve.Fori(0, PAIRS) as p:
                        it = b * PAIRS + p
                        for q in range(2):
                            wait_reg(dve, xt_done, it * 2 + (q + 1))
                            TT(xg[:, 4 * q:4 * q + 4, :], bank[:, q, :].rearrange("p (k c) -> p k c", k=4),
                               bc(g_ffn[:, 4 * q:4 * q + 4], P), ALU.mult).then_inc(xg_ready, 1)
                        for e in range(2):
                            wait_reg(dve, silu_done, it * 2 + (e + 1))
                            rows = slice(CAP * e, CAP * e + CAP)
                            TT(hid[rows, :], silu[rows, :], bank[rows, 3, :], ALU.mult).then_inc(act_ready, 1)
                    STT(wnow[:, :, :], place[:, ROUND_, :, :], 0.0, rs[:, 4:6, :].rearrange("p k t -> p t k"),
                        ALU.is_equal, ALU.mult).then_inc(w_round, 1)
                    wait_reg(dve, w_round, b * 2 + 1)
                    for k in range(2):
                        for t in range(NT):
                            wait_reg(dve, y_tok[2 * t + k], b * 16 + 16)
                            if k:
                                wait_reg(dve, comb_step, b * 8 + (t + 1))
                            STT(x[:, t, :], ytok[2 * t + k], wnow[:, t, k:k + 1], x[:, t, :], ALU.mult, ALU.add)\
                                .then_inc(comb_step, 1)
                    TS(place[:, ROUND_, :, :], place[:, ROUND_, :, :], 1.0, None, ALU.subtract).then_inc(w_round, 1)
                    wait_reg(dve, comb_step, b * 8 + 8)
                    wait_reg(dve, w_round, b * 2 + 2)
                    dve.sem_inc(combined, 1)
                close_layer(dve, l)


_INS = ['x', 'positions', 'norm_mix', 'norm_ffn', 'w_in', 'q_gain', 'k_gain', 'cmp_k_pos', 'cmp_k_w1', 'cmp_k_w2',
        'cmp_v_pos', 'cmp_v_w1', 'cmp_v_w2', 's5_a_re', 's5_a_im', 's5_log_dt', 's5_b_re', 's5_b_im', 's5_c_re',
        's5_c_im', 's5_d', 's5_glu', 'proj_nsa', 'proj_s5', 'w_out', 'router_group', 'router_group_bias',
        'router_expert', 'router_expert_bias', 'expert_gate', 'expert_up', 'expert_down']


def kernel(**inputs):
    import numpy as _np
    import concourse.bacc as _bacc
    from concourse import mybir as _mybir
    from concourse.bass_utils import run_bass_kernel_spmd as _run

    nc = _bacc.Bacc("TRN2", target_bir_lowering=False, num_devices=1)
    arrays, aps = {}, {}
    for name in _INS:
        v = _np.ascontiguousarray(inputs[name])
        if name.startswith("expert_"):
            v = v.reshape(v.shape[0] * v.shape[1], v.shape[2], v.shape[3])
        arrays[f"in_{name}"] = v
        aps[name] = nc.dram_tensor(f"in_{name}", v.shape, _mybir.dt.from_np(v.dtype), kind="ExternalInput").ap()
    out = nc.dram_tensor("out_0", (1, 512, 1024), _mybir.dt.float32, kind="ExternalOutput").ap()
    trunk(nc, aps, out)
    r = _run(nc, [arrays], core_ids=[0])
    return r.results[0]["out_0"]
```
